# Optimizing a Trainium2 kernel written in Bass

```python
import math
import jax
import jax.numpy as jnp
from jax import lax
import numpy as np

D_MODEL = 2048
BATCH = 1
SEQ = 256
DEPTH = 2

BRANCH_W = D_MODEL // 2
N_BRANCH = 4
CHUNK = 64
EPS = 1e-6
GDN_HEADS = 8
GDN_DK = BRANCH_W // GDN_HEADS
GDN_CONV = 4
GDN_QKV = 3 * BRANCH_W
HGRN_HEADS = 8
HGRN_DK = BRANCH_W // HGRN_HEADS
S5_GROUP = 16
S5_GROUPS = BRANCH_W // S5_GROUP
S5_STATE = 64
RET_HEADS = 8
RET_DK = BRANCH_W // RET_HEADS
ROPE_BASE = 10000.0
MAX_START = 4096
GATE_COLS = N_BRANCH * D_MODEL
SPLIT_SIZES = (GDN_QKV, GDN_HEADS, GDN_HEADS, BRANCH_W,
               BRANCH_W, BRANCH_W, BRANCH_W, BRANCH_W,
               BRANCH_W, BRANCH_W,
               BRANCH_W, BRANCH_W, BRANCH_W, BRANCH_W,
               GATE_COLS)
N_IN = sum(SPLIT_SIZES)

kernel_name = 'hybrid_gdn_hgrn2_s5_retention_gated_merge'

def rmsnorm(x, w):
    xf = x.astype(jnp.float32)
    y = xf * lax.rsqrt(jnp.mean(xf * xf, axis=-1, keepdims=True) + EPS)
    return (y * w.astype(jnp.float32)).astype(x.dtype)

def l2norm(x):
    return x * lax.rsqrt(jnp.sum(x * x, axis=-1, keepdims=True) + EPS)

def masked_exp(mask, logv):
    return jnp.where(mask, jnp.exp(jnp.where(mask, logv, 0.0)), 0.0)

def head_rmsnorm_gate(o, w, z):
    B, L = o.shape[0], o.shape[1]
    o = o * lax.rsqrt(jnp.mean(o * o, axis=-1, keepdims=True) + EPS) * w.astype(jnp.float32)
    return o.reshape(B, L, -1) * jax.nn.silu(z)

def to_chunks(x):
    B, L, H, d = x.shape
    return x.reshape(B, L // CHUNK, CHUNK, H, d).transpose(0, 3, 1, 2, 4)

def from_chunks(o):
    B, H, N, C, d = o.shape
    return o.transpose(0, 2, 3, 1, 4).reshape(B, N * C, H, d)

def causal_conv(x, w):
    K = w.shape[-1]
    rhs = jnp.transpose(w)[:, None, :]
    return lax.conv_general_dilated(x, rhs, window_strides=(1,), padding=[(K - 1, 0)],
                                    dimension_numbers=('NWC', 'WIO', 'NWC'),
                                    feature_group_count=x.shape[-1])

def rope(x, positions):
    half = x.shape[-1] // 2
    inv = ROPE_BASE ** (-jnp.arange(half, dtype=jnp.float32) / half)
    ang = positions.astype(jnp.float32)[..., None] * inv
    cos = jnp.cos(ang)[:, :, None, :]
    sin = jnp.sin(ang)[:, :, None, :]
    x1, x2 = x[..., :half], x[..., half:]
    return jnp.concatenate([x1 * cos - x2 * sin, x1 * sin + x2 * cos], axis=-1)

def gated_delta_rule(q, k, v, beta, g):
    B, H, N, C, dk = q.shape
    dv = v.shape[-1]
    gc = jnp.cumsum(g, axis=-1)
    causal = jnp.tril(jnp.ones((C, C), dtype=bool))
    strict = jnp.tril(jnp.ones((C, C), dtype=bool), -1)
    diff = gc[..., :, None] - gc[..., None, :]
    decay = masked_exp(causal, diff)
    kb = k * beta[..., None]
    a_mat = jnp.where(strict, jnp.einsum('bhnid,bhnjd->bhnij', kb, k) * decay, 0.0)
    eye = jnp.eye(C, dtype=q.dtype)
    rhs = jnp.concatenate([v * beta[..., None], kb * jnp.exp(gc)[..., None]], axis=-1)
    sol = lax.linalg.triangular_solve(eye + a_mat, rhs, left_side=True, lower=True,
                                      unit_diagonal=True)
    u, w = sol[..., :dv], sol[..., dv:]
    attn = jnp.einsum('bhnid,bhnjd->bhnij', q, k) * decay
    q_dec = q * jnp.exp(gc)[..., None]
    k_dec = k * jnp.exp(gc[..., -1:] - gc)[..., None]
    g_tot = jnp.exp(gc[..., -1])

    def step(state, xs):
        u_c, w_c, qd_c, kd_c, attn_c, gt_c = xs
        v_new = u_c - jnp.einsum('bhcd,bhde->bhce', w_c, state)
        o_c = (jnp.einsum('bhcd,bhde->bhce', qd_c, state)
               + jnp.einsum('bhij,bhje->bhie', attn_c, v_new))
        state = state * gt_c[..., None, None] + jnp.einsum('bhcd,bhce->bhde', kd_c, v_new)
        return state, o_c

    xs = tuple(jnp.moveaxis(t, 2, 0) for t in (u, w, q_dec, k_dec, attn, g_tot))
    state0 = jnp.zeros((B, H, dk, dv), q.dtype)
    _, o = lax.scan(step, state0, xs)
    return jnp.moveaxis(o, 0, 2)

def hgrn2_chunked(q, k, v, log_f):
    B, H, N, C, dk = q.shape
    dv = v.shape[-1]
    gc = jnp.cumsum(log_f, axis=-2)
    causal = jnp.tril(jnp.ones((C, C), dtype=bool))[:, :, None]

    def step(state, xs):
        q_c, k_c, v_c, gc_c = xs
        diff = gc_c[:, :, :, None, :] - gc_c[:, :, None, :, :]
        dec = masked_exp(causal, diff)
        attn = jnp.einsum('bhid,bhjd,bhijd->bhij', q_c, k_c, dec)
        o_c = (jnp.einsum('bhid,bhde->bhie', q_c * jnp.exp(gc_c), state)
               + jnp.einsum('bhij,bhje->bhie', attn, v_c))
        g_last = gc_c[:, :, -1]
        state = (state * jnp.exp(g_last)[..., None]
                 + jnp.einsum('bhcd,bhce->bhde', k_c * jnp.exp(g_last[:, :, None] - gc_c), v_c))
        return state, o_c

    xs = tuple(jnp.moveaxis(t, 2, 0) for t in (q, k, v, gc))
    state0 = jnp.zeros((B, H, dk, dv), q.dtype)
    _, o = lax.scan(step, state0, xs)
    return jnp.moveaxis(o, 0, 2)

def retention_chunked(q, k, v, log_gamma):
    C = q.shape[-2]
    idx = jnp.arange(C, dtype=jnp.float32)
    diff = idx[:, None] - idx[None, :]
    lg = log_gamma[:, None, None]
    dmask = masked_exp(diff >= 0, lg * diff)
    scores = jnp.einsum('bhnid,bhnjd->bhnij', q, k) * dmask[None, :, None]
    o_intra = jnp.einsum('bhnij,bhnje->bhnie', scores, v)
    k_dec = k * jnp.exp(log_gamma[:, None] * (C - 1 - idx))[None, :, None, :, None]
    chunk_kv = jnp.einsum('bhncd,bhnce->bhnde', k_dec, v)
    chunk_decay = jnp.exp(log_gamma * C)[None, :, None, None]

    def step(r, kv):
        return r * chunk_decay + kv, r

    _, r_prev = lax.scan(step, jnp.zeros_like(chunk_kv[:, :, 0]), jnp.moveaxis(chunk_kv, 2, 0))
    r_prev = jnp.moveaxis(r_prev, 0, 2)
    q_dec = q * jnp.exp(log_gamma[:, None] * (idx + 1.0))[None, :, None, :, None]
    o_inter = jnp.einsum('bhnid,bhnde->bhnie', q_dec, r_prev)
    return o_intra + o_inter

def _linear_combine(e1, e2):
    a1, b1 = e1
    a2, b2 = e2
    return a1 * a2, a2 * b1 + b2

def gdn_branch(qkv, b, a, z, conv_w, a_log, dt_bias, norm_w):
    B, L, _ = qkv.shape
    qkv = jax.nn.silu(causal_conv(qkv, conv_w.astype(jnp.float32)))
    q, k, v = jnp.split(qkv, 3, axis=-1)
    q = l2norm(q.reshape(B, L, GDN_HEADS, GDN_DK)) * (GDN_DK ** -0.5)
    k = l2norm(k.reshape(B, L, GDN_HEADS, GDN_DK))
    v = v.reshape(B, L, GDN_HEADS, GDN_DK)
    beta = jax.nn.sigmoid(b)
    g = -jnp.exp(a_log.astype(jnp.float32)) * jax.nn.softplus(a + dt_bias.astype(jnp.float32))
    o = gated_delta_rule(to_chunks(q), to_chunks(k), to_chunks(v),
                         to_chunks(beta[..., None])[..., 0], to_chunks(g[..., None])[..., 0])
    return head_rmsnorm_gate(from_chunks(o), norm_w, z)

def hgrn2_branch(q, f_logit, i_in, g, lb, norm_w):
    B, L, _ = q.shape
    lb = lb.astype(jnp.float32)
    q = jax.nn.silu(q)
    log_f = jnp.log(lb + (1.0 - lb) * jax.nn.sigmoid(f_logit))
    k = (1.0 - lb) * jax.nn.sigmoid(-f_logit)
    shp = (B, L, HGRN_HEADS, HGRN_DK)
    o = hgrn2_chunked(to_chunks(q.reshape(shp)), to_chunks(k.reshape(shp)),
                      to_chunks(i_in.reshape(shp)), to_chunks(log_f.reshape(shp)))
    return head_rmsnorm_gate(from_chunks(o), norm_w, g)

def s5_branch(u, z, lam_re, lam_im, log_dt, b_re, b_im, c_re, c_im, d, glu_w, glu_b):
    B, L, W = u.shape
    f32 = jnp.float32
    lam = lax.complex(lam_re.astype(f32), lam_im.astype(f32))
    dt = jnp.exp(log_dt.astype(f32))[:, None]
    lam_bar = jnp.exp(lam * dt)
    b_bar = ((lam_bar - 1.0) / lam)[..., None] * lax.complex(b_re.astype(f32), b_im.astype(f32))
    ug = u.reshape(B, L, S5_GROUPS, S5_GROUP).astype(jnp.complex64)
    bu = jnp.einsum('blgc,gpc->lbgp', ug, b_bar)
    a = jnp.broadcast_to(lam_bar, (L, 1) + lam_bar.shape)
    _, states = lax.associative_scan(_linear_combine, (a, bu), axis=0)
    c = lax.complex(c_re.astype(f32), c_im.astype(f32))
    y = jnp.einsum('lbgp,gcp->blgc', states, c).real.reshape(B, L, W) + d.astype(f32) * u
    y = jax.nn.gelu(y)
    y = y * jax.nn.sigmoid(jnp.einsum('blw,wv->blv', y, glu_w.astype(f32)) + glu_b.astype(f32))
    return y * jax.nn.silu(z)

def retention_branch(q, k, v, g, positions, log_gamma):
    B, L, _ = q.shape
    shp = (B, L, RET_HEADS, RET_DK)
    q = rope(q.reshape(shp), positions)
    k = rope(k.reshape(shp), positions) * (RET_DK ** -0.5)
    v = v.reshape(shp)
    o = from_chunks(retention_chunked(to_chunks(q), to_chunks(k), to_chunks(v), log_gamma))
    mu = jnp.mean(o, axis=-1, keepdims=True)
    var = jnp.mean(jnp.square(o - mu), axis=-1, keepdims=True)
    o = (o - mu) * lax.rsqrt(var + EPS)
    return o.reshape(B, L, -1) * jax.nn.silu(g)

def setup_inputs(seed: int = 0) -> dict:
    key = jax.random.key(seed)
    ks = iter(jax.random.split(key, 32))
    f32 = jnp.float32

    def nrm(shape, scale):
        return jax.random.normal(next(ks), shape, f32) * scale

    def unif(shape, lo, hi):
        return jax.random.uniform(next(ks), shape, f32, lo, hi)

    Ld = DEPTH
    x = nrm((BATCH, SEQ, D_MODEL), 1.0)
    start = jax.random.randint(next(ks), (BATCH, 1), 0, MAX_START, dtype=jnp.int32)
    positions = start + jnp.arange(SEQ, dtype=jnp.int32)[None, :]
    norm_w = 1.0 + nrm((Ld, D_MODEL), 0.02)
    w_in = nrm((Ld, D_MODEL, N_IN), D_MODEL ** -0.5)
    gdn_conv_w = nrm((Ld, GDN_QKV, GDN_CONV), GDN_CONV ** -0.5)
    gdn_a_log = jnp.log(unif((Ld, GDN_HEADS), 1.0, 16.0))
    dt = jnp.exp(unif((Ld, GDN_HEADS), math.log(1e-3), math.log(1e-1)))
    gdn_dt_bias = dt + jnp.log(-jnp.expm1(-dt))
    gdn_norm_w = 1.0 + nrm((Ld, GDN_DK), 0.02)
    hgrn_lb_logits = 1.0 + nrm((Ld, BRANCH_W), 0.1)
    hgrn_norm_w = 1.0 + nrm((Ld, HGRN_DK), 0.02)
    s5_lambda_re = -0.5 + nrm((Ld, S5_GROUPS, S5_STATE), 0.01)
    s5_lambda_im = math.pi * jnp.arange(S5_STATE, dtype=f32) + nrm((Ld, S5_GROUPS, S5_STATE), 0.01)
    s5_log_dt = unif((Ld, S5_GROUPS), math.log(1e-3), math.log(1e-1))
    s5_b_re = nrm((Ld, S5_GROUPS, S5_STATE, S5_GROUP), (2.0 * S5_GROUP) ** -0.5)
    s5_b_im = nrm((Ld, S5_GROUPS, S5_STATE, S5_GROUP), (2.0 * S5_GROUP) ** -0.5)
    s5_c_re = nrm((Ld, S5_GROUPS, S5_GROUP, S5_STATE), S5_STATE ** -0.5)
    s5_c_im = nrm((Ld, S5_GROUPS, S5_GROUP, S5_STATE), S5_STATE ** -0.5)
    s5_d = nrm((Ld, BRANCH_W), 1.0)
    s5_glu_w = nrm((Ld, BRANCH_W, BRANCH_W), BRANCH_W ** -0.5)
    s5_glu_b = nrm((Ld, BRANCH_W), 0.01)
    w_branch = nrm((Ld, N_BRANCH, BRANCH_W, D_MODEL), BRANCH_W ** -0.5)
    w_out = nrm((Ld, D_MODEL, D_MODEL), 0.5 * D_MODEL ** -0.5)
    final_norm_w = 1.0 + nrm((D_MODEL,), 0.02)
    return {'x': x, 'positions': positions, 'norm_w': norm_w, 'w_in': w_in,
            'gdn_conv_w': gdn_conv_w, 'gdn_a_log': gdn_a_log, 'gdn_dt_bias': gdn_dt_bias,
            'gdn_norm_w': gdn_norm_w, 'hgrn_lb_logits': hgrn_lb_logits, 'hgrn_norm_w': hgrn_norm_w,
            's5_lambda_re': s5_lambda_re, 's5_lambda_im': s5_lambda_im, 's5_log_dt': s5_log_dt,
            's5_b_re': s5_b_re, 's5_b_im': s5_b_im, 's5_c_re': s5_c_re, 's5_c_im': s5_c_im,
            's5_d': s5_d, 's5_glu_w': s5_glu_w, 's5_glu_b': s5_glu_b,
            'w_branch': w_branch, 'w_out': w_out, 'final_norm_w': final_norm_w}

def reference(x, positions, norm_w, w_in, gdn_conv_w, gdn_a_log, gdn_dt_bias, gdn_norm_w,
              hgrn_lb_logits, hgrn_norm_w, s5_lambda_re, s5_lambda_im, s5_log_dt,
              s5_b_re, s5_b_im, s5_c_re, s5_c_im, s5_d, s5_glu_w, s5_glu_b,
              w_branch, w_out, final_norm_w):
    f32 = jnp.float32
    B, L, _ = x.shape
    p_lb = jax.nn.softmax(hgrn_lb_logits.astype(f32), axis=0)
    lower_bounds = jnp.cumsum(p_lb, axis=0) - p_lb[0]
    ret_log_gamma = jnp.log1p(-jnp.exp2(-5.0 - jnp.arange(RET_HEADS, dtype=f32)))
    split_idx = [int(s) for s in np.cumsum(SPLIT_SIZES)[:-1]]

    for l in range(DEPTH):
        h = rmsnorm(x, norm_w[l])
        proj = jnp.einsum('bld,dn->bln', h, w_in[l]).astype(f32)
        (gdn_qkv, gdn_b, gdn_a, gdn_z, hg_q, hg_f, hg_i, hg_g, s5_u, s5_z,
         ret_q, ret_k, ret_v, ret_g, gate_logits) = jnp.split(proj, split_idx, axis=-1)

        y_a = gdn_branch(gdn_qkv, gdn_b, gdn_a, gdn_z, gdn_conv_w[l], gdn_a_log[l],
                         gdn_dt_bias[l], gdn_norm_w[l])
        y_b = hgrn2_branch(hg_q, hg_f, hg_i, hg_g, lower_bounds[l], hgrn_norm_w[l])
        y_c = s5_branch(s5_u, s5_z, s5_lambda_re[l], s5_lambda_im[l], s5_log_dt[l],
                        s5_b_re[l], s5_b_im[l], s5_c_re[l], s5_c_im[l], s5_d[l],
                        s5_glu_w[l], s5_glu_b[l])
        y_d = retention_branch(ret_q, ret_k, ret_v, ret_g, positions, ret_log_gamma)

        ys = jnp.stack([y_a, y_b, y_c, y_d], axis=2).astype(x.dtype)
        branch = jnp.einsum('blcw,cwd->blcd', ys, w_branch[l]).astype(f32)
        gates = jax.nn.sigmoid(gate_logits.reshape(B, L, N_BRANCH, D_MODEL))
        merged = jnp.sum(gates * branch, axis=2)
        x = x + jnp.einsum('bld,de->ble', merged.astype(x.dtype), w_out[l])

    return rmsnorm(x, final_norm_w)


_drawn_inputs = setup_inputs


def setup_inputs(seed=0):
    import zlib

    import numpy as np

    out = dict(_drawn_inputs(seed))
    spreads = {}
    factors = {'norm_w': 4.053,
     'gdn_norm_w': 8.0,
     'hgrn_lb_logits': 8.0,
     'hgrn_norm_w': 8.0,
     's5_lambda_re': 64.0,
     's5_lambda_im': 64.0,
     's5_log_dt': 64.0,
     's5_b_re': 64.0,
     's5_b_im': 64.0,
     's5_c_re': 64.0,
     's5_c_im': 64.0,
     's5_glu_b': 64.0,
     'final_norm_w': 7.976}
    for name, (base, spread) in spreads.items():
        noise = np.random.default_rng([zlib.crc32(name.encode()), seed]).standard_normal(out[name].shape)
        drawn = base * np.exp(spread * noise) if base else spread * noise
        out[name] = jnp.asarray(drawn.astype(out[name].dtype))
    for name, factor in factors.items():
        out[name] = (out[name] * factor).astype(out[name].dtype)
    return out
```

```python
import math
from contextlib import ExitStack

import numpy as np
import concourse.bass as bass
from concourse import mybir

P = 128
D_MODEL, SEQ, DEPTH = 2048, 256, 2
BRANCH_W = D_MODEL // 2
UNITS = BRANCH_W // P
KT = D_MODEL // P
KB = BRANCH_W // P
EPS = 1e-6
DK_SCALE = float(P) ** -0.5
CONV = 4
S5_GROUP, S5_STATE = 16, 64
S5_GROUPS = BRANCH_W // S5_GROUP
ST = 4
STATE_TILES = ST * UNITS
MT = D_MODEL // P
N_BRANCH = 4
SPLIT = (3 * BRANCH_W, UNITS, UNITS, BRANCH_W, BRANCH_W, BRANCH_W, BRANCH_W, BRANCH_W, BRANCH_W, BRANCH_W,
         BRANCH_W, BRANCH_W, BRANCH_W, BRANCH_W, N_BRANCH * D_MODEL)
OFF = [sum(SPLIT[:i]) for i in range(len(SPLIT))]
N_IN = sum(SPLIT)
GQ, GK, GV = 0, BRANCH_W, 2 * BRANCH_W
(GAB, GZ, HQ, HF, HI, HG, SU, SZ, RQ, RK, RV, RG, GATES) = (
    OFF[1], OFF[3], OFF[4], OFF[5], OFF[6], OFF[7], OFF[8], OFF[9], OFF[10], OFF[11], OFF[12], OFF[13], OFF[14])
BLOCKS = (HF, GK, GQ, GV, SU, HQ, HI, RQ, RK, RV, GZ, HG, SZ, RG)
(B_HF, B_GK, B_GQ, B_GV, B_SU, B_HQ, B_HI, B_RQ, B_RK, B_RV, B_GZ, B_HG, B_SZ, B_RG) = range(14)
NB = len(BLOCKS)
HALF = 8
UNIT_SLOTS = 7
USES = 2 * NB // UNIT_SLOTS
TAIL_SLOTS = 4
MERGE_ORDER = (0, 1, 3, 2)
GLU_USES = UNITS // TAIL_SLOTS
MERGE_USES = 3 * N_BRANCH // TAIL_SLOTS
OUT_TILES = 2
TAIL_USES = GLU_USES + MT * MERGE_USES + MT // OUT_TILES
LEVELS = 7
NEG = -1.0e30
TWO_PI = 2.0 * math.pi
SIN_TURN = 6.283185
MAGIC = 12582912.0
C1, C2 = 6.28125, 1.9352436065673828e-3
C3 = TWO_PI - C1 - C2
V_NORM, V_LB0, V_LB1, V_S5D, V_GLUB, V_GNW, V_HNW, V_FNW = 0, 16, 24, 32, 40, 48, 49, 50
V_ROWS = 66
(C_NGC0, C_SUF0, C_NGC1, C_GC0, C_GC1, C_BETA0, C_BETA1) = range(7)
NCOL = 7
GA_N, GB_N, HA_N, RA_N, SA_N = 21, 3, 11, 3, 4

INPUTS = ['x', 'positions', 'norm_w', 'w_in', 'gdn_conv_w', 'gdn_a_log', 'gdn_dt_bias', 'gdn_norm_w',
          'hgrn_lb_logits', 'hgrn_norm_w', 's5_lambda_re', 's5_lambda_im', 's5_log_dt', 's5_b_re', 's5_b_im',
          's5_c_re', 's5_c_im', 's5_d', 's5_glu_w', 's5_glu_b', 'w_branch', 'w_out', 'final_norm_w']


def shape_constants():
    f = np.float32
    i = np.arange(P)
    row, col = i[:, None], i[None, :]
    squares = np.stack([
        np.eye(P),
        row <= col,
        -1.0 * (row <= col),
        row > col,
        np.where(col >= row, 0.0, NEG),
        np.where(row > col, 0.0, NEG),
    ], axis=1).astype(f)
    lower = np.stack([((row ^ col) >> s == 1) & (row > col) for s in range(LEVELS)], axis=1)
    upper = np.stack([row == col] + [((row ^ col) >> s == 1) & (col > row) for s in range(LEVELS)], axis=1)
    gamma = np.log1p(-np.exp2(-5.0 - np.arange(UNITS)))[None, :, None]
    ahead = (np.arange(SEQ)[None, :] - i[:, None])[:, None, :]
    ret = np.where(ahead >= 0, np.exp(gamma * np.maximum(ahead, 0)) * DK_SCALE, 0.0).astype(f)
    half = P // 2
    inv = (10000.0 ** (-(np.arange(half, dtype=f)) / f(half))).astype(f)
    sign = np.where(i < half, -1.0, 1.0)
    cols = np.zeros((P, 4), f)
    cols[:, 0] = inv[i % half]
    cols[:, 1] = sign
    even = ((i // S5_GROUP) % 2 == 0).astype(f)
    cmask = np.zeros((P, 2, 2, S5_STATE), f)
    for part, s in ((0, 1.0), (1, -1.0)):
        cmask[:, part, 0] = s * even[:, None]
        cmask[:, part, 1] = s * (1 - even)[:, None]
    steps = np.broadcast_to(np.arange(SEQ, dtype=f) - SEQ // 2, (P, SEQ)).copy()
    lsel = np.zeros((P, DEPTH), f)
    lsel[:, 1:] = 1.0
    return {
        "c_squares": squares, "c_masks": np.concatenate([lower, upper], axis=1).astype(f), "c_ret": ret,
        "c_cols": cols, "c_cmask": cmask.reshape(P, 2, 2 * S5_STATE), "c_steps": steps, "c_lsel": lsel,
    }


def trunk_kernel(nc, A, out):
    f32, u8, i32 = mybir.dt.float32, mybir.dt.uint8, mybir.dt.int32
    ALU, ACT, AX = mybir.AluOpType, mybir.ActivationFunctionType, mybir.AxisListType
    ds = bass.ds
    ctx = ExitStack()
    with ctx:
        def sb(name, shape, dt=f32):
            return ctx.enter_context(nc.sbuf_tensor(name, shape, dt))

        def bank(name):
            return ctx.enter_context(nc.psum_tensor(name, [P, 512], f32))

        def sem(name):
            return ctx.enter_context(nc.semaphore(name))

        xT = sb("xT", [P, KT, SEQ])
        hT = sb("hT", [P, KT, SEQ])
        yT = sb("yT", [P, N_BRANCH, UNITS, SEQ])
        zs = sb("zs", [P, UNITS, SEQ])
        unit_w = [sb(f"unit_w{s}", [P, HALF, P]) for s in range(UNIT_SLOTS)]
        tail_w = [sb(f"tail_w{s}", [P, HALF, P]) for s in range(TAIL_SLOTS)]
        region = sb("region", [P, 6 * 4 * SEQ])
        s5_view = region[:, :].rearrange("p (a t n) -> p a t n", a=6, t=ST)
        s5_cos, s5_sin, s5_re, s5_im, s5_p, s5_q = (s5_view[:, a] for a in range(6))
        merged = region[:, 0:MT * SEQ].rearrange("p (t n) -> p t n", n=SEQ)
        squares = merged
        lam_t = region[0:STATE_TILES, 4096:5632].rearrange("p (a n) -> p a n", a=12)
        s5_rows = region[0:STATE_TILES, 5632:6144].rearrange("p (a n) -> p a n", a=4)
        masks_in = region[:, 4096:4096 + (2 * LEVELS + 1) * P].rearrange("p (a n) -> p a n", n=P)
        x_tok = region[:, 0:2 * D_MODEL].rearrange("p (a n) -> p a n", a=2)
        sq = sb("sq", [P, 6, P])
        ident, upto, neg_upto, after, mask_dt, mask_ds = (sq[:, a, :] for a in range(6))
        masks = sb("masks", [P, 2 * LEVELS + 1, P], u8)
        lower, upper = masks[:, 0:LEVELS, :], masks[:, LEVELS:, :]
        ret_decay = sb("ret_decay", [P, UNITS, SEQ])
        ccols = sb("ccols", [P, 4])
        cmask = sb("cmask", [P, 2, 2 * S5_STATE])
        steps = sb("steps", [P, SEQ])
        lsel = sb("lsel", [P, DEPTH])
        ones = sb("ones", [P, P])
        mhalf = sb("mhalf", [P, 4])
        eps_p = sb("eps_p", [P, 2])
        x_rs = sb("x_rs", [P, 2])
        rope_cos = sb("rope_cos", [P, SEQ])
        rope_sin = sb("rope_sin", [P, SEQ])
        vec_rows = sb("vec_rows", [V_ROWS, P])
        vec = sb("vec", [P, V_ROWS])
        conv_w = sb("conv_w", [P, 3 * UNITS, CONV])
        a_log = sb("a_log", [P, UNITS])
        dt_bias = sb("dt_bias", [P, UNITS])
        w_ab = sb("w_ab", [P, KT, 2 * UNITS])
        ab = sb("ab", [P, 2, 2 * UNITS])
        gate_g = sb("gate_g", [P, 2, UNITS])
        gate_t = sb("gate_t", [P, 4, 2, UNITS])
        unit_cols = sb("unit_cols", [P, UNITS, NCOL])
        lb = sb("lb", [P, UNITS, 2])
        lb_t = sb("lb_t", [P, 4, UNITS])
        lam = sb("lam", [STATE_TILES, 2, P])
        log_dt = sb("log_dt", [STATE_TILES, 2])
        s5_par = sb("s5_par", [P, 4, STATE_TILES])
        rms = sb("rms", [P, SEQ])
        conv_in = [sb(f"conv_in{n}", [P, CONV - 1 + SEQ]) for n in range(3)]
        gk, gq, gv = (sb(n, [P, SEQ]) for n in ("gk", "gq", "gv"))
        gk2, gq2 = s5_re[:, 0, :], s5_im[:, 0, :]
        junk, h_o, g_o, r_o = (v.rearrange("p (a n) -> p a n", a=2) for v in (
            s5_re[:, 1, :], s5_re[:, 2, :], s5_re[:, 3, :], s5_im[:, 1, :]))
        gcols = sb("gcols", [P, NCOL])
        g_bc = sb("g_bc", [P, 2, P])
        dec_t = sb("dec_t", [P, 3, P])
        dec_s = sb("dec_s", [P, 2, P])
        gnorm = sb("gnorm", [P, 4])
        gfac = sb("gfac", [P, 12])
        am = sb("am", [P, 2, P])
        kx = sb("kx", [P, P])
        xm = [sb(f"xm{n}", [P, 2, P]) for n in range(2)]
        tt = sb("tt", [P, 4, P])
        rr = sb("rr", [P, 2, P])
        g_att = sb("g_att", [P, 3, P])
        vb = sb("vb", [P, 2, P])
        vn = sb("vn", [P, 2, P])
        vt = sb("vt", [P, P])
        g_ms = sb("g_ms", [P, 4])
        hsig = sb("hsig", [P, 2, SEQ])
        hf = sb("hf", [P, SEQ])
        hq = sb("hq", [P, SEQ])
        hk = sb("hk", [P, SEQ])
        hv = sb("hv", [P, 2, P])
        h_att = sb("h_att", [P, 3, P])
        h_ms = sb("h_ms", [P, 4])
        rx = [sb(f"rx{n}", [P, SEQ]) for n in range(2)]
        rsw = [sb(f"rsw{n}", [P, SEQ]) for n in range(2)]
        rv = sb("rv", [P, 2, P])
        r_att = sb("r_att", [P, 3, P])
        r_st = sb("r_st", [P, 2, 6])
        r_mv = sb("r_mv", [P, 2, 2])
        r_rs = sb("r_rs", [P, 2])
        s_u = sb("s_u", [P, SEQ])
        b_raw = sb("b_raw", [P, 2, ST, S5_GROUP])
        c_raw = sb("c_raw", [P, 2, S5_STATE])
        b_t = sb("b_t", [P, 4, ST, S5_GROUP])
        bc_pad = sb("bc_pad", [P, 4, P])
        bc_T = sb("bc_T", [P, 4, P])
        s_thr = sb("s_thr", [P, 2, ST])
        gate_s = [conv_in[n][:, CONV - 1:] for n in range(2)]
        prod = gv

        glu_s = (s5_view[:, 5, 0, :], s5_view[:, 5, 1, :])

        PJ = [bank("PJ0"), bank("PJ1")]
        GA, GB, HA, RA = (bank(n) for n in ("GA", "GB", "HA", "RA"))
        S2 = ctx.enter_context(nc.psum_tensor("S2", [P, 2, 512], f32))
        SA, SB = S2[:, 0, :], S2[:, 1, :]

        consts_in, x_in, x_out = sem("consts_in"), sem("x_in"), sem("x_out")
        params_in, params_used = sem("params_in"), sem("params_used")
        unit_full = [sem(f"unit_full{s}") for s in range(UNIT_SLOTS)]
        unit_used = [sem(f"unit_used{s}") for s in range(UNIT_SLOTS)]
        tail_full = [sem(f"tail_full{s}") for s in range(TAIL_SLOTS)]
        tail_used = [sem(f"tail_used{s}") for s in range(TAIL_SLOTS)]
        bc_in, bc_used, bc_padded = sem("bc_in"), sem("bc_used"), sem("bc_padded")
        vec_rowsT, vec_ready = sem("vec_rowsT"), sem("vec_ready")
        s5_rows_ready, s5_rowsT, s5_par_ready = sem("s5_rows_ready"), sem("s5_rowsT"), sem("s5_par_ready")
        xT_written, xT_read = sem("xT_written"), sem("xT_read")
        x_ready = sem("x_ready")
        diag_ready, rms_spread = sem("diag_ready"), sem("rms_spread")
        sq_ready, ms_written, ms_ready, rms_ready, h_ready = (
            sem("sq_ready"), sem("ms_written"), sem("ms_ready"), sem("rms_ready"), sem("h_ready"))
        ab_written, ab_ready, act_p, dve_p = sem("ab_written"), sem("ab_ready"), sem("act_p"), sem("dve_p")
        g_ready, gc_written, cols_ready = sem("g_ready"), sem("gc_written"), sem("cols_ready")
        pj_read = sem("pj_read")
        ga_w, ga_r = sem("ga_written"), sem("ga_read")
        gb_w, gb_r = sem("gb_written"), sem("gb_read")
        ha_w, ha_r = sem("ha_written"), sem("ha_read")
        ra_w, ra_r = sem("ra_written"), sem("ra_read")
        sa_w, sa_r = sem("sa_written"), sem("sa_read")
        gcols_ready = sem("gcols_ready")
        conv_staged, conv_summed, conv_done = sem("conv_staged"), sem("conv_summed"), sem("conv_done")
        gdn_qkv_used = sem("gdn_qkv_used")
        gsum_ready, gnorm_ready = sem("gsum_ready"), sem("gnorm_ready")
        g_ms_ready, g_rs_ready = sem("g_ms_ready"), sem("g_rs_ready")
        h_ms_ready, h_rs_ready = sem("h_ms_ready"), sem("h_rs_ready")
        r_var_ready, r_rs_ready = sem("r_var_ready"), sem("r_rs_ready")
        hsig_staged, hsig_used = sem("hsig_staged"), sem("hsig_used")
        hq_staged, hv_staged, hgrn_used = sem("hq_staged"), sem("hv_staged"), sem("hgrn_used")
        rope_staged, roped, rv_staged, ret_used = (
            sem("rope_staged"), sem("roped"), sem("rv_staged"), sem("ret_used"))
        u_staged, s5_used = sem("u_staged"), sem("s5_used")
        phase_ready, sincos_ready, x_re_im_ready = sem("phase_ready"), sem("sincos_ready"), sem("x_re_im_ready")
        gz_staged, hz_staged, rz_staged = sem("gz_staged"), sem("hz_staged"), sem("rz_staged")
        units_done = sem("units_done")
        gelu_done, glu_sig, glu_done = sem("gelu_done"), sem("glu_sig"), sem("glu_done")
        gate_r, br_r, out_r = sem("gate_read"), sem("branch_read"), sem("out_read")
        rope_ready, rope_done = sem("rope_ready"), sem("rope_done")

        W = A["w_in"].rearrange("l (k p) n -> l p k n", p=P)
        WB = A["w_branch"].rearrange("l c (k p) n -> l c p k n", p=P)
        WO = A["w_out"].rearrange("l (k p) n -> l p k n", p=P)
        WG = A["s5_glu_w"].rearrange("l (k p) n -> l p k n", p=P)
        XV = A["x"].rearrange("b (a p) n -> (b p) a n", p=P)
        OV = out.rearrange("b (a p) n -> (b p) a n", p=P)

        block = ctx.enter_context(nc.Block())

        @block.sync
        def _(sp):
            for name, dst in (("c_squares", sq[:, :, :]), ("c_masks", masks_in), ("c_ret", ret_decay[:, :, :]),
                              ("c_cmask", cmask[:, :, :])):
                sp.dma_start(dst, A[name]).then_inc(consts_in, 16)
            for name, dst in (("c_cols", ccols), ("c_steps", steps), ("c_lsel", lsel)):
                sp.dma_start(dst[:, :], A[name]).then_inc(consts_in, 16)
            with sp.Fori(0, DEPTH) as l:
                with sp.Fori(0, UNITS) as u:
                    n0 = sp.snap((l * UNITS + u) * USES)
                    for i in range(2 * NB):
                        s, n, b, k0 = i % UNIT_SLOTS, i // UNIT_SLOTS, i // 2, (i % 2) * HALF
                        sp.wait_ge(unit_used[s], n0 + (n + 1))
                        sp.dma_start(unit_w[s][:, :, :],
                                     W[ds(l, 1), :, k0:k0 + HALF, ds(u * P + BLOCKS[b], P)].rearrange(
                                         "l p k n -> (l p) k n")).then_inc(unit_full[s], 16)
                t0 = sp.snap(l * TAIL_USES)

                def load_tail(i, base, source):
                    s, n = i % TAIL_SLOTS, i // TAIL_SLOTS
                    sp.wait_ge(tail_used[s], base + (n + 1))
                    sp.dma_start(tail_w[s][:, :, :], source).then_inc(tail_full[s], 16)

                with sp.Fori(0, GLU_USES) as g:
                    base = sp.snap(t0 + g)
                    for i in range(TAIL_SLOTS):
                        load_tail(i, base, WG[ds(l, 1), :, :, ds(g * (TAIL_SLOTS * P) + i * P, P)].rearrange(
                            "l p k n -> (l p) k n"))
                with sp.Fori(0, MT) as t:
                    base = sp.snap(t0 + GLU_USES + t * MERGE_USES)
                    for m, c in enumerate(MERGE_ORDER):
                        for h in range(2):
                            load_tail(3 * m + h, base,
                                      W[ds(l, 1), :, h * HALF:(h + 1) * HALF,
                                        ds(t * P + (GATES + c * D_MODEL), P)].rearrange("l p k n -> (l p) k n"))
                        load_tail(3 * m + 2, base, WB[ds(l, 1), c, :, :, ds(t * P, P)].rearrange(
                            "l p k n -> (l p) k n"))
                with sp.Fori(0, MT // OUT_TILES) as t:
                    base = sp.snap(t0 + (GLU_USES + MT * MERGE_USES) + t)
                    for i in range(2 * OUT_TILES):
                        h = i % 2
                        load_tail(i, base, WO[ds(l, 1), :, h * HALF:(h + 1) * HALF,
                                              ds(t * (OUT_TILES * P) + (i // 2) * P, P)].rearrange(
                                                  "l p k n -> (l p) k n"))
            sp.wait_ge(x_out, 16)

        @block.gpsimd
        def _(pool):
            for s in (pj_read, gate_r, br_r, out_r, glu_sig, glu_done):
                pool.sem_inc(s, 2)
            for s in (unit_used + tail_used + [ga_r, gb_r, ha_r, ra_r, sa_r, gdn_qkv_used, hgrn_used, ret_used,
                                               s5_used, bc_used, hsig_used, params_used]):
                pool.sem_inc(s, 1)
            with pool.Fori(0, DEPTH) as l:
                l1 = pool.snap(l + 1)
                pool.wait_ge(params_used, l1)
                rows = [(V_NORM, A["norm_w"][ds(l, 1), :], 16), (V_LB0, A["hgrn_lb_logits"][0:1, :], 8),
                        (V_LB1, A["hgrn_lb_logits"][1:2, :], 8), (V_S5D, A["s5_d"][ds(l, 1), :], 8),
                        (V_GLUB, A["s5_glu_b"][ds(l, 1), :], 8), (V_GNW, A["gdn_norm_w"][ds(l, 1), :], 1),
                        (V_HNW, A["hgrn_norm_w"][ds(l, 1), :], 1)]
                for r, src, n in rows:
                    pool.dma_start(vec_rows[r:r + n, :], src.rearrange("l (t p) -> (l t) p", p=P)).then_inc(
                        params_in, 16)
                pool.dma_start(vec_rows[V_FNW:V_FNW + 16, :],
                               A["final_norm_w"].rearrange("(t p) -> t p", p=P)).then_inc(params_in, 16)
                pool.dma_start(conv_w[:, :, :], A["gdn_conv_w"][ds(l, 1), :, :].rearrange(
                    "l (t p) k -> (l p) t k", p=P)).then_inc(params_in, 16)
                pool.dma_start(a_log[:, :], A["gdn_a_log"][ds(l, 1), :].to_broadcast([P, UNITS])).then_inc(
                    params_in, 16)
                pool.dma_start(dt_bias[:, :], A["gdn_dt_bias"][ds(l, 1), :].to_broadcast([P, UNITS])).then_inc(
                    params_in, 16)
                pool.dma_start(w_ab[:, :, :], W[ds(l, 1), :, :, GAB:GAB + 2 * UNITS].rearrange(
                    "l p k n -> (l p) k n")).then_inc(params_in, 16)
                for n, name in enumerate(("s5_lambda_re", "s5_lambda_im")):
                    pool.dma_start(lam[:, n, :], A[name][ds(l, 1), :, :].rearrange(
                        "l (j g) p -> (l j) (g p)", g=2)).then_inc(params_in, 16)
                pool.dma_start(log_dt[:, :], A["s5_log_dt"][ds(l, 1), :].rearrange(
                    "l (j g) -> (l j) g", g=2)).then_inc(params_in, 16)

                pool.wait_ge(ms_ready, l1)
                nc.gpsimd.tensor_tensor(x_rs[:, :], x_rs[:, :], mhalf[:, 0:2], ALU.pow).then_inc(rms_ready, 1)
                with pool.Fori(0, UNITS) as u:
                    n1 = pool.snap(l * UNITS + u + 1)
                    pool.wait_ge(bc_used, n1)
                    pool.wait_ge(s5_par_ready, l1)
                    for n, name in enumerate(("s5_b_re", "s5_b_im")):
                        for j in range(ST):
                            pool.dma_start(b_raw[:, n, j, :], A[name][ds(l, 1), ds(u * (2 * ST) + 2 * j, 2), :, :]
                                           .rearrange("l g p c -> (l g p) c")).then_inc(bc_in, 16)
                    for n, name in enumerate(("s5_c_re", "s5_c_im")):
                        pool.dma_start(c_raw[:, n, :], A[name][ds(l, 1), ds(u * (2 * ST), 2 * ST), :, :].rearrange(
                            "l g c p -> (l g c) p")).then_inc(bc_in, 16)
                    pool.wait_ge(bc_in, n1 * (16 * (2 * ST + 2)))
                    scale = [s5_par[:, 2 + n, ds(u * ST, ST)].unsqueeze(2).to_broadcast([P, ST, S5_GROUP])
                             for n in range(2)]
                    for a, (n, m) in enumerate(((0, 0), (1, 1), (0, 1), (1, 0))):
                        nc.gpsimd.tensor_tensor(b_t[:, a], b_raw[:, n], scale[m], ALU.mult)
                    cview = bc_pad[:, 2:4, :].rearrange("p n (g s) -> p n g s", g=2)
                    for n in range(2):
                        nc.gpsimd.tensor_tensor(
                            cview[:, n], c_raw[:, n, :].unsqueeze(1).to_broadcast([P, 2, S5_STATE]),
                            cmask[:, n, :].rearrange("p (g s) -> p g s", g=2), ALU.mult)
                    pool.drain()
                    bview = bc_pad[:, 0:2, :].rearrange("p n (j g c) -> p n j g c", j=ST, g=2)
                    last = None
                    for g in range(2):
                        rows_g = slice(64 * g, 64 * g + 64)
                        nc.gpsimd.tensor_tensor(bview[rows_g, 0, :, g, :], b_t[rows_g, 0], b_t[rows_g, 1],
                                                ALU.subtract)
                        last = nc.gpsimd.tensor_tensor(bview[rows_g, 1, :, g, :], b_t[rows_g, 2], b_t[rows_g, 3],
                                                       ALU.add)
                    last.then_inc(bc_padded, 1)
                    pool.wait_ge(gsum_ready, n1)
                    nc.gpsimd.tensor_tensor(gnorm[:, :], gnorm[:, :], mhalf[:, 0:4], ALU.pow).then_inc(
                        gnorm_ready, 1)

                    def inverse_root(ms):
                        nc.gpsimd.tensor_tensor(ms[:, 2:4], ms[:, 0:2], eps_p[:, :], ALU.add)
                        pool.drain()
                        nc.gpsimd.tensor_tensor(ms[:, 2:4], ms[:, 2:4], mhalf[:, 0:2], ALU.pow)
                        pool.drain()
                        return nc.gpsimd.tensor_scalar(ms[:, 2:4], ms[:, 2:4], math.sqrt(P), 1.0, ALU.mult, ALU.mult)

                    pool.wait_ge(h_ms_ready, n1)
                    inverse_root(h_ms).then_inc(h_rs_ready, 1)
                    pool.wait_ge(r_var_ready, n1)
                    nc.gpsimd.tensor_tensor(r_rs[:, :], r_rs[:, :], mhalf[:, 0:2], ALU.pow).then_inc(r_rs_ready, 1)
                    pool.wait_ge(g_ms_ready, n1)
                    inverse_root(g_ms)
                    pool.drain()
                    nc.gpsimd.tensor_tensor(g_ms[:, 2:4], g_ms[:, 2:4], gfac[:, 6:8], ALU.mult).then_inc(
                        g_rs_ready, 1)
            pool.wait_ge(ms_ready, DEPTH + 1)
            nc.gpsimd.tensor_tensor(x_rs[:, :], x_rs[:, :], mhalf[:, 0:2], ALU.pow).then_inc(rms_ready, 1)

        @block.scalar
        def _(act):
            A_ = nc.scalar.activation
            act.dma_start(x_tok[:, :, :], XV).then_inc(x_in, 16)
            act.dma_start(hf[:, :].bitcast(i32), A["positions"].to_broadcast([P, SEQ])).then_inc(x_in, 16)
            act.wait_ge(rope_ready, 1)
            A_(rope_sin[:, :], rms[:, :], ACT.Sin, scale=SIN_TURN)
            A_(rope_cos[:, :], rms[:, :], ACT.Sin, scale=SIN_TURN / 2)
            act.drain()
            A_(rope_cos[:, :], rope_cos[:, :], ACT.Square, scale=math.sqrt(2.0))
            act.drain().then_inc(rope_done, 1)

            def square_x():
                for k in range(0, KT, 4):
                    last = A_(squares[:, k:k + 4, :], xT[:, k:k + 4, :], ACT.Square)
                last.then_inc(sq_ready, 1)

            with act.Fori(0, DEPTH) as l:
                l1 = act.snap(l + 1)
                act.wait_ge(x_ready, l1)
                square_x()
                act.wait_ge(params_in, l1 * (16 * 15))
                A_(log_dt[:, :], log_dt[:, :], ACT.Exp).then_inc(act_p, 1)
                act.wait_ge(dve_p, l * 4 + 1)
                A_(s5_rows[:, 0, :], lam_t[:, 0, :], ACT.Exp)
                A_(lam_t[:, 2, :], lam_t[:, 0, :], ACT.Tanh, scale=0.5).then_inc(act_p, 1)
                act.wait_ge(dve_p, l * 4 + 2)
                A_(lb_t[:, 0:2, :], lb_t[:, 0:2, :], ACT.Exp).then_inc(act_p, 1)
                act.wait_ge(dve_p, l * 4 + 3)
                A_(gate_t[:, 0], ab[:, :, 0:UNITS], ACT.Exp, scale=-1.0)
                A_(gate_t[:, 2], gate_t[:, 2], ACT.Exp, scale=-1.0)
                A_(a_log[:, :], a_log[:, :], ACT.Exp)
                act.drain()
                A_(gate_t[:, 2], gate_t[:, 2], ACT.Ln, bias=1.0).then_inc(act_p, 1)
                act.wait_ge(dve_p, l * 4 + 4)
                A_(lam_t[:, 3, :], s5_rows[:, 1, :], ACT.Sin, scale=SIN_TURN)
                A_(lam_t[:, 4, :], s5_rows[:, 1, :], ACT.Sin, scale=SIN_TURN / 2).then_inc(act_p, 1)

                with act.Fori(0, UNITS) as u:
                    n = act.snap(l * UNITS + u)
                    n1 = act.snap(n + 1)
                    n0, ga0, gb0 = act.snap(n * USES), act.snap(n * GA_N), act.snap(n * GB_N)
                    ha0, sa0, cv0 = act.snap(n * HA_N), act.snap(n * SA_N), act.snap(n * 3)

                    def projected(b):
                        act.wait_ge(unit_used[(2 * b + 1) % UNIT_SLOTS], n0 + ((2 * b + 1) // UNIT_SLOTS + 2))
                        return PJ[b % 2][:, 0:SEQ]

                    def decays():
                        act.wait_ge(gb_w, gb0 + 1)
                        for a, c in enumerate((C_NGC0, C_SUF0, C_NGC1)):
                            last = A_(dec_t[:, a, :], GB[:, a * P:(a + 1) * P], ACT.Exp, bias=gcols[:, c:c + 1])
                        last.then_inc(gb_r, 1)
                        act.wait_ge(gb_w, gb0 + 2)
                        for a, c in enumerate((C_GC0, C_GC1)):
                            last = A_(dec_s[:, a, :], GB[:, a * P:(a + 1) * P], ACT.Exp, bias=gcols[:, c:c + 1])
                        last.then_inc(gb_r, 1)

                    def stage_conv(b, m):
                        src = projected(b)
                        A_(conv_in[m][:, CONV - 1:], src, ACT.Copy)
                        A_((gk, gq, gv)[m][:, :], src, ACT.Copy, scale=tap(m, CONV - 1)).then_inc(pj_read, 1)

                    def tap(m, k):
                        part = (1, 0, 2)[m]
                        return conv_w[:, ds(u + part * UNITS, 1), k:k + 1].rearrange("p a b -> p (a b)")

                    def silu_conv(m, square=None):
                        act.wait_ge(conv_summed, cv0 + (m + 1))
                        t = (gk, gq, gv)[m]
                        last = A_(t[:, :], t[:, :], ACT.Silu)
                        if square is not None:
                            act.drain()
                            last = A_(square, t[:, :], ACT.Square)
                        last.then_inc(conv_done, 1)

                    def square_sums(src, ms, scale):
                        for a in range(2):
                            last = A_(junk[:, a, :], src[:, a * P:(a + 1) * P], ACT.Square,
                                      scale=scale[a], accum_out=ms[:, a:a + 1])
                        return last

                    act.wait_ge(hsig_used, n1)
                    act.wait_ge(gcols_ready, n1)
                    act.wait_ge(gdn_qkv_used, n1)
                    decays()
                    src = projected(B_HF)
                    A_(hsig[:, 0, :], src, ACT.Exp, scale=-1.0)
                    A_(hsig[:, 1, :], src, ACT.Exp).then_inc(pj_read, 1)
                    act.drain().then_inc(hsig_staged, 1)
                    stage_conv(B_GK, 0)
                    act.drain().then_inc(conv_staged, 1)
                    act.wait_ge(sa_w, sa0 + 1)
                    A_(bc_T[:, :, :], SA, ACT.Copy).then_inc(sa_r, 1)
                    stage_conv(B_GQ, 1)
                    act.drain().then_inc(conv_staged, 1)
                    silu_conv(0, gk2)
                    silu_conv(1, gq2)
                    stage_conv(B_GV, 2)
                    act.drain().then_inc(conv_staged, 1)
                    act.wait_ge(phase_ready, n1)
                    A_(s5_sin, s5_p, ACT.Sin, scale=SIN_TURN)
                    A_(s5_cos, s5_p, ACT.Sin, scale=SIN_TURN / 2)
                    act.drain()
                    A_(s5_cos, s5_cos, ACT.Square, scale=math.sqrt(2.0)).then_inc(sincos_ready, 1)
                    silu_conv(2)
                    act.wait_ge(s5_used, n1)
                    A_(s_u[:, :], projected(B_SU), ACT.Copy).then_inc(pj_read, 1)
                    act.drain().then_inc(u_staged, 1)
                    act.wait_ge(hgrn_used, n1)
                    A_(hq[:, :], projected(B_HQ), ACT.Silu).then_inc(pj_read, 1)
                    act.drain().then_inc(hq_staged, 1)
                    A_(hv[:, :, :], projected(B_HI), ACT.Copy).then_inc(pj_read, 1)
                    act.drain().then_inc(hv_staged, 1)
                    act.wait_ge(ret_used, n1)
                    for m, b in enumerate((B_RQ, B_RK)):
                        src = projected(b)
                        A_(rx[m][:, :], src, ACT.Copy)
                        A_(rsw[m][0:64, :], src[64:128, :], ACT.Copy)
                        A_(rsw[m][64:128, :], src[0:64, :], ACT.Copy).then_inc(pj_read, 1)
                        act.drain().then_inc(rope_staged, 1)
                    A_(rv[:, :, :], projected(B_RV), ACT.Copy).then_inc(pj_read, 1)
                    act.drain().then_inc(rv_staged, 1)
                    def gate_of(branch):
                        return yT[:, branch, ds(u, 1), :].rearrange("p a n -> p (a n)")

                    A_(gate_of(0), projected(B_GZ), ACT.Silu).then_inc(pj_read, 1)
                    act.drain().then_inc(gz_staged, 1)
                    act.wait_ge(ha_w, ha0 + 10)
                    square_sums(HA, h_ms, (1.0, 1.0))
                    act.drain().then_inc(h_ms_ready, 1)
                    A_(gate_of(1), projected(B_HG), ACT.Silu).then_inc(pj_read, 1)
                    act.drain().then_inc(hz_staged, 1)
                    act.wait_ge(h_rs_ready, n1)
                    for a in range(2):
                        last = A_(h_o[:, a, :], HA[:, a * P:(a + 1) * P], ACT.Copy, scale=h_ms[:, 2 + a:3 + a])
                    last.then_inc(ha_r, 1)
                    A_(zs[:, ds(u, 1), :].rearrange("p a n -> p (a n)"), projected(B_SZ), ACT.Silu).then_inc(
                        pj_read, 1)
                    act.wait_ge(ga_w, ga0 + 20)
                    square_sums(GA, g_ms, (gfac[:, 6:7], gfac[:, 7:8]))
                    act.drain().then_inc(g_ms_ready, 1)
                    A_(gate_of(3), projected(B_RG), ACT.Silu).then_inc(pj_read, 1)
                    act.drain().then_inc(rz_staged, 1)
                    act.wait_ge(g_rs_ready, n1)
                    for a in range(2):
                        last = A_(g_o[:, a, :], GA[:, a * P:(a + 1) * P], ACT.Copy, scale=g_ms[:, 2 + a:3 + a])
                    last.then_inc(ga_r, 1)

                act.wait_ge(units_done, l1 * UNITS)
                for k in range(0, UNITS, 4):
                    last = A_(yT[:, 2, k:k + 4, :], yT[:, 2, k:k + 4, :], ACT.Gelu_apprx_tanh)
                last.then_inc(gelu_done, 1)
                t0 = act.snap(l * TAIL_USES)
                with act.Fori(0, GLU_USES) as g:
                    n = act.snap((l * GLU_USES + g) * TAIL_SLOTS)
                    base = act.snap(t0 + g)
                    for i in range(TAIL_SLOTS):
                        act.wait_ge(tail_used[i], base + 2)
                        act.wait_ge(glu_done, n + (i + 1))
                        A_(glu_s[i % 2], PJ[i % 2][:, 0:SEQ], ACT.Sigmoid,
                           bias=vec[:, ds(g * TAIL_SLOTS + (V_GLUB + i), 1)]).then_inc(glu_sig, 1)
                with act.Fori(0, MT) as t:
                    n = act.snap((l * MT + t) * N_BRANCH)
                    base = act.snap(t0 + GLU_USES + t * MERGE_USES)
                    for m in range(N_BRANCH):
                        i = 3 * m + 1
                        act.wait_ge(tail_used[i % TAIL_SLOTS], base + (i // TAIL_SLOTS + 2))
                        act.wait_ge(br_r, n + (m + 1))
                        A_(gate_s[m % 2], PJ[m % 2][:, 0:SEQ], ACT.Sigmoid).then_inc(gate_r, 1)
            act.wait_ge(x_ready, DEPTH + 1)
            square_x()
            act.wait_ge(xT_read, KT // 2 + 2 * KT // 4)
            act.dma_start(OV, x_tok).then_inc(x_out, 16)

        @block.vector
        def _(dve):
            TS, TT, STT = nc.vector.tensor_scalar, nc.vector.tensor_tensor, nc.vector.scalar_tensor_tensor
            CP = nc.vector.tensor_copy

            for n in range(3):
                nc.vector.memset(conv_in[n][:, 0:CONV - 1], 0.0)
            nc.vector.memset(h_att[:, :, :], 0.0)
            nc.vector.memset(bc_pad[:, :, :], 0.0)
            nc.vector.memset(ones[:, :], 1.0)
            nc.vector.memset(mhalf[:, :], -0.5)
            nc.vector.memset(eps_p[:, :], EPS * P)
            pos_i = hf[:, :].bitcast(i32)
            dve.wait_ge(x_in, 32)
            CP(hq[:, :], pos_i)
            dve.wait_ge(consts_in, 16 * 7)
            CP(masks[:, :, :], masks_in)
            dve.drain()

            def reduce_turns(dst, angle, n_buf):
                TS(n_buf, angle, 1.0 / TWO_PI, MAGIC, ALU.mult, ALU.add)
                dve.drain()
                TS(n_buf, n_buf, MAGIC, None, ALU.subtract)
                dve.drain()
                for c in (C1, C2, C3):
                    STT(angle, n_buf, -c, angle, ALU.mult, ALU.add)
                    dve.drain()
                TS(dst, angle, 1.0 / TWO_PI, 0.5, ALU.mult, ALU.min)
                dve.drain()
                return TS(dst, dst, -0.5, None, ALU.max)

            TS(hq[:, :], hq[:, :], ccols[:, 0:1], None, ALU.mult)
            dve.drain()
            reduce_turns(rms[:, :], hq[:, :], hk[:, :]).then_inc(rope_ready, 1)
            dve.wait_ge(rope_done, 1)
            TS(rope_cos[:, :], rope_cos[:, :], -1.0, 1.0, ALU.mult, ALU.add)
            TS(rope_sin[:, :], rope_sin[:, :], ccols[:, 1:2], None, ALU.mult)
            with dve.Fori(0, KT // 2) as k:
                n = dve.snap(k)
                dve.wait_ge(xT_written, n + 1)
                CP(xT[:, ds(k * 2, 2), :], GA[:, :].rearrange("p (a n) -> p a n", a=2)).then_inc(xT_read, 1)
            dve.drain().then_inc(x_ready, 1)

            def mean_square():
                TS(x_rs[:, :], GA[:, 0:2], 1.0 / D_MODEL, EPS, ALU.mult, ALU.add).then_inc(ms_ready, 1)

            def diagonal(n):
                dve.wait_ge(rms_ready, n)
                for a in range(2):
                    TS(am[:, a, :], ident, x_rs[:, a:a + 1], None, ALU.mult)
                dve.drain().then_inc(diag_ready, 1)
                dve.wait_ge(rms_spread, n)

            with dve.Fori(0, DEPTH) as l:
                l1 = dve.snap(l + 1)
                a0 = dve.snap(l * 5)
                dve.wait_ge(ms_written, l1)
                mean_square()
                dve.wait_ge(vec_rowsT, l1)
                CP(vec[:, :], GB[:, 0:V_ROWS]).then_inc(vec_ready, 1)
                dve.drain()
                diagonal(l1)
                for k in range(KT):
                    last = STT(hT[:, k, :], xT[:, k, :], vec[:, V_NORM + k:V_NORM + k + 1], GA[:, 0:SEQ],
                               ALU.mult, ALU.mult)
                last.then_inc(h_ready, 1)
                L = lambda a: lam_t[:, a, :]
                dve.wait_ge(act_p, a0 + 1)
                dtb = log_dt[:, :].unsqueeze(2).to_broadcast([STATE_TILES, 2, S5_STATE])
                v3 = lambda ap: ap.rearrange("p (g s) -> p g s", g=2)
                TT(v3(L(0)), v3(lam[:, 0, :]), dtb, ALU.mult)
                TT(v3(L(1)), v3(lam[:, 1, :]), dtb, ALU.mult)
                dve.drain().then_inc(dve_p, 1)
                reduce_turns(s5_rows[:, 1, :], L(1), L(5))
                dve.wait_ge(vec_ready, l1)
                V0, V1 = vec[:, V_LB0:V_LB0 + UNITS], vec[:, V_LB1:V_LB1 + UNITS]
                TT(lb_t[:, 2, :], V0, V1, ALU.max)
                dve.drain()
                TT(lb_t[:, 0, :], V0, lb_t[:, 2, :], ALU.subtract)
                TT(lb_t[:, 1, :], V1, lb_t[:, 2, :], ALU.subtract).then_inc(dve_p, 1)
                dve.wait_ge(ab_written, l1)
                CP(ab[:, :, :], RA[:, 0:4 * UNITS].rearrange("p (a n) -> p a n", a=2))
                dve.drain()
                TT(gate_t[:, 1], ab[:, :, UNITS:2 * UNITS],
                   dt_bias[:, :].unsqueeze(1).to_broadcast([P, 2, UNITS]), ALU.add)
                dve.drain()
                TS(gate_t[:, 3], gate_t[:, 1], 0.0, None, ALU.max)
                STT(gate_t[:, 2], gate_t[:, 1], -1.0, gate_t[:, 1], ALU.mult, ALU.max)
                dve.drain().then_inc(dve_p, 1)
                dve.drain().then_inc(dve_p, 1)
                dve.wait_ge(act_p, a0 + 3)
                TT(lb_t[:, 2, :], lb_t[:, 0, :], lb_t[:, 1, :], ALU.add)
                dve.drain()
                nc.vector.reciprocal(lb_t[:, 2, :], lb_t[:, 2, :])
                dve.drain()
                TT(lb_t[:, 0, :], lb_t[:, 0, :], lb_t[:, 2, :], ALU.mult)
                TT(lb_t[:, 1, :], lb_t[:, 1, :], lb_t[:, 2, :], ALU.mult)
                dve.drain()
                STT(lb_t[:, 1, :], lb_t[:, 1, :], lsel[:, ds(l, 1)], lb_t[:, 0, :], ALU.mult, ALU.add)
                dve.drain()
                TT(lb[:, :, 0], lb_t[:, 1, :], lb_t[:, 0, :], ALU.subtract)
                dve.drain()
                TS(lb[:, :, 1], lb[:, :, 0], -1.0, 1.0, ALU.mult, ALU.add)
                dve.wait_ge(act_p, a0 + 4)
                TS(gate_t[:, 0], gate_t[:, 0], 1.0, None, ALU.add)
                TT(gate_t[:, 3], gate_t[:, 3], gate_t[:, 2], ALU.add)
                dve.drain()
                beta_out = unit_cols[:, :, C_BETA0:C_BETA1 + 1].rearrange("p u a -> p a u")
                nc.vector.reciprocal(beta_out, gate_t[:, 0])
                STT(gate_g[:, :, :], gate_t[:, 3], -1.0, a_log[:, :].unsqueeze(1).to_broadcast([P, 2, UNITS]),
                    ALU.mult, ALU.mult).then_inc(g_ready, 1)
                dve.wait_ge(gc_written, l1)
                G16 = RA[:, 0:2 * UNITS].rearrange("p (a u) -> p u a", a=2)
                TS(unit_cols[:, :, C_GC0:C_GC1 + 1], G16, 1.0, None, ALU.mult)
                TS(unit_cols[:, :, C_NGC0:C_NGC1 + 1:2], G16, -1.0, None, ALU.mult)
                TS(unit_cols[:, :, C_SUF0], RA[:, 2 * UNITS:3 * UNITS], 1.0, None, ALU.mult)
                dve.drain().then_inc(cols_ready, 1)
                dve.wait_ge(act_p, a0 + 5)
                TS(L(2), L(2), 0.5, None, ALU.min)
                TT(L(5), L(4), L(4), ALU.mult)
                TS(L(6), L(0), 0.5, None, ALU.is_gt)
                TS(L(7), s5_rows[:, 0, :], -1.0, None, ALU.add)
                TT(L(10), lam[:, 0, :], lam[:, 0, :], ALU.mult)
                TT(L(11), lam[:, 1, :], lam[:, 1, :], ALU.mult)
                dve.drain()
                TS(L(8), L(2), -1.0, 1.0, ALU.mult, ALU.add)
                TS(L(5), L(5), -2.0, None, ALU.mult)
                TT(L(10), L(10), L(11), ALU.add)
                dve.drain()
                nc.vector.reciprocal(L(8), L(8))
                nc.vector.reciprocal(L(10), L(10))
                dve.drain()
                STT(L(8), L(2), 2.0, L(8), ALU.mult, ALU.mult)
                dve.drain()
                TT(L(7), L(7), L(8), ALU.subtract)
                dve.drain()
                TT(L(7), L(7), L(6), ALU.mult)
                dve.drain()
                TT(L(8), L(8), L(7), ALU.add)
                TS(L(9), L(5), 1.0, None, ALU.add)
                TT(L(3), L(3), s5_rows[:, 0, :], ALU.mult)
                dve.drain()
                TT(L(8), L(8), L(9), ALU.mult)
                dve.drain()
                TT(L(8), L(8), L(5), ALU.add)
                dve.drain()
                TT(L(5), L(8), lam[:, 0, :], ALU.mult)
                TT(L(6), L(3), lam[:, 1, :], ALU.mult)
                TT(L(7), L(3), lam[:, 0, :], ALU.mult)
                TT(L(9), L(8), lam[:, 1, :], ALU.mult)
                dve.drain()
                TT(L(5), L(5), L(6), ALU.add)
                TT(L(7), L(7), L(9), ALU.subtract)
                dve.drain()
                TT(s5_rows[:, 2, :], L(5), L(10), ALU.mult)
                TT(s5_rows[:, 3, :], L(7), L(10), ALU.mult)
                dve.drain().then_inc(s5_rows_ready, 1)
                dve.wait_ge(s5_rowsT, l1)
                CP(s5_par[:, :, :], RA[:, 0:4 * STATE_TILES].rearrange("p (a n) -> p a n", a=4))
                dve.drain().then_inc(s5_par_ready, 1)

                with dve.Fori(0, UNITS) as u:
                    n = dve.snap(l * UNITS + u)
                    n1 = dve.snap(n + 1)
                    ga0, gb0, ha0 = dve.snap(n * GA_N), dve.snap(n * GB_N), dve.snap(n * HA_N)
                    ra0, sa0, cv0 = dve.snap(n * RA_N), dve.snap(n * SA_N), dve.snap(n * 3)

                    def tap(m, k):
                        part = (1, 0, 2)[m]
                        return conv_w[:, ds(u + part * UNITS, 1), k:k + 1].rearrange("p a b -> p (a b)")

                    def conv_taps(m):
                        dve.wait_ge(conv_staged, cv0 + (m + 1))
                        t = (gk, gq, gv)[m]
                        for k in range(CONV - 2, -1, -1):
                            last = STT(t[:, :], conv_in[m][:, k:k + SEQ], tap(m, k), t[:, :], ALU.mult, ALU.add)
                            if k:
                                dve.drain()
                        last.then_inc(conv_summed, 1)

                    def level_mask(s, dst):
                        TT(dst[:, :, :], am[:, :, :], lower[:, s, :].unsqueeze(1).to_broadcast([P, 2, P]), ALU.mult)

                    dve.wait_ge(gdn_qkv_used, n1)
                    CP(gcols[:, :], unit_cols[:, ds(u, 1), :].rearrange("p a c -> p (a c)"))
                    for a in range(2):
                        last = CP(g_bc[:, a, :], gate_g[:, a, ds(u, 1)].to_broadcast([P, P]))
                    dve.drain().then_inc(gcols_ready, 1)
                    for j in range(ST):
                        TS(s5_p[:, j, :], steps[:, :], s5_par[:, 1, ds(u * ST + j, 1)], None, ALU.mult)
                    dve.drain()
                    TS(s5_q, s5_p, MAGIC, MAGIC, ALU.add, ALU.subtract)
                    dve.drain()
                    TT(s5_p, s5_p, s5_q, ALU.subtract).then_inc(phase_ready, 1)
                    dve.wait_ge(hsig_staged, n1)
                    TS(hsig[:, :, :], hsig[:, :, :], 1.0, None, ALU.add)
                    dve.drain()
                    nc.vector.reciprocal(hsig[:, :, :], hsig[:, :, :])
                    dve.drain()
                    dve.wait_ge(hgrn_used, n1)
                    lb0, lb1 = (lb[:, ds(u, 1), c:c + 1].rearrange("p a b -> p (a b)") for c in range(2))
                    TS(hf[:, :], hsig[:, 0, :], lb1, lb0, ALU.mult, ALU.add)
                    TS(hk[:, :], hsig[:, 1, :], lb1, None, ALU.mult)
                    dve.drain().then_inc(hsig_used, 1)
                    conv_taps(0)
                    conv_taps(1)
                    dve.wait_ge(ga_w, ga0 + 1)
                    TS(gnorm[:, :], GA[:, 0:4], EPS, None, ALU.add)
                    dve.drain().then_inc(gsum_ready, 1)
                    conv_taps(2)
                    dve.wait_ge(gnorm_ready, n1)
                    TT(gfac[:, 0:2], gnorm[:, 0:2], gcols[:, C_BETA0:C_BETA1 + 1], ALU.mult)
                    TS(gfac[:, 6:8], gnorm[:, 2:4], DK_SCALE, None, ALU.mult).then_inc(ga_r, 1)
                    dve.drain()
                    TT(gfac[:, 2:4], gfac[:, 0:2], gnorm[:, 0:2], ALU.mult)
                    dve.drain()
                    TS(gfac[:, 4:6], gfac[:, 2:4], -1.0, None, ALU.mult)
                    dve.wait_ge(ga_w, ga0 + 2)
                    dve.wait_ge(gb_r, gb0 + 3)
                    for a in range(2):
                        STT(am[:, a, :], GA[:, a * P:(a + 1) * P], gfac[:, 2 + a:3 + a], dec_s[:, a, :],
                            ALU.mult, ALU.mult)
                    TT(kx[:, :], GA[:, 2 * P:3 * P], dec_t[:, 1, :], ALU.mult).then_inc(ga_r, 1)
                    dve.drain()
                    dve.wait_ge(gb_w, gb0 + 3)
                    for a in range(2):
                        last = TS(vb[:, a, :], GB[:, a * P:(a + 1) * P], gfac[:, a:a + 1], None, ALU.mult)
                    last.then_inc(gb_r, 1)
                    level_mask(0, xm[0])
                    dve.wait_ge(ga_w, ga0 + 3)
                    TT(g_att[:, :, :].rearrange("p a n -> p (a n)"), GA[:, 0:3 * P],
                       dec_t[:, :, :].rearrange("p a n -> p (a n)"), ALU.mult)
                    dve.drain().then_inc(ga_r, 1)
                    TT(tt[:, 0:2, :], ident.unsqueeze(1).to_broadcast([P, 2, P]), xm[0][:, :, :], ALU.subtract)
                    level_mask(1, xm[1])
                    dve.wait_ge(ga_w, ga0 + 4)
                    STT(tt[:, 2:4, :], GA[:, 0:2 * P].rearrange("p (a n) -> p a n", a=2), -1.0,
                        ident.unsqueeze(1).to_broadcast([P, 2, P]), ALU.mult, ALU.add)
                    dve.drain().then_inc(ga_r, 1)

                    def invert(s):
                        dve.wait_ge(ga_w, ga0 + (5 + 2 * (s - 1)))
                        CP(rr[:, :, :].rearrange("p a n -> p (a n)"), GA[:, 0:2 * P])
                        dve.drain().then_inc(ga_r, 1)
                        if s + 1 < LEVELS:
                            level_mask(s + 1, xm[(s + 1) % 2])
                        dve.wait_ge(ga_w, ga0 + (6 + 2 * (s - 1)))
                        first = 0 if s + 1 < LEVELS else 2
                        TT(tt[:, first:4, :].rearrange("p a n -> p (a n)"),
                           tt[:, first:4, :].rearrange("p a n -> p (a n)"), GA[:, first * P:4 * P], ALU.subtract)
                        dve.drain().then_inc(ga_r, 1)

                    def s5_rotate(half):
                        j = slice(2 * half, 2 * half + 2)
                        re, im = S2[:, :, 0:SEQ], S2[:, :, SEQ:2 * SEQ]
                        dve.wait_ge(sa_w, sa0 + (2 + half))
                        TT(s5_p[:, 0:2], re, s5_cos[:, j], ALU.mult)
                        TT(s5_q[:, 0:2], im, s5_sin[:, j], ALU.mult)
                        TT(s5_p[:, 2:4], im, s5_cos[:, j], ALU.mult)
                        TT(s5_q[:, 2:4], re, s5_sin[:, j], ALU.mult).then_inc(sa_r, 1)
                        dve.drain()
                        TT(s5_re[:, j], s5_p[:, 0:2], s5_q[:, 0:2], ALU.add)
                        TT(s5_im[:, j], s5_p[:, 2:4], s5_q[:, 2:4], ALU.subtract)
                        dve.drain()

                    def s5_scan(half):
                        for j in range(2 * half, 2 * half + 2):
                            mag = s5_par[:, 0, ds(u * ST + j, 1)].to_broadcast([P, SEQ])
                            for v in (s5_re, s5_im):
                                nc.vector.tensor_tensor_scan(v[:, j, :], mag, v[:, j, :], 0.0, ALU.mult, ALU.add)

                    def s5_back():
                        dve.drain()
                        TT(s5_p, s5_re, s5_cos, ALU.mult)
                        TT(s5_q, s5_im, s5_sin, ALU.mult)
                        dve.drain()
                        TT(s5_p, s5_p, s5_q, ALU.subtract)
                        TT(s5_re, s5_re, s5_sin, ALU.mult)
                        TT(s5_im, s5_im, s5_cos, ALU.mult)
                        dve.drain()
                        TT(s5_q, s5_im, s5_re, ALU.add)
                        dve.drain().then_inc(x_re_im_ready, 1)

                    def h_scores(stage, h):
                        dve.wait_ge(ha_w, ha0 + (stage + 1))
                        if stage == 0:
                            TT(hq[:, :], hq[:, :], hf[:, :], ALU.mult)
                        else:
                            s = 1 << (stage - 1)
                            tot = hf[:, 0:SEQ:s].rearrange("p (b two) -> p b two", two=2)
                            nblk = SEQ // (2 * s)
                            q2 = hq[:, :].rearrange("p (b two s) -> p b two s", two=2, s=s)[:, :, 1, :]
                            k2 = hk[:, :].rearrange("p (b two s) -> p b two s", two=2, s=s)[:, :, 0, :]
                            TT(q2, q2, tot[:, :, 0:1].to_broadcast([P, nblk, s]), ALU.mult)
                            TT(k2, k2, tot[:, :, 1:2].to_broadcast([P, nblk, s]), ALU.mult)
                            dve.drain()
                            TT(hf[:, 0:SEQ:2 * s], tot[:, :, 0], tot[:, :, 1], ALU.mult)
                        nc.vector.copy_predicated(
                            h_att[:, 0:3:2, :], upper[:, stage, :].unsqueeze(1).to_broadcast([P, 2, P]),
                            HA[:, 0:2 * P].rearrange("p (a n) -> p a n", a=2))
                        dve.drain().then_inc(ha_r, 1)

                    def rope(m):
                        dve.wait_ge(rope_staged, n * 2 + (m + 1))
                        TT(rx[m][:, :], rx[m][:, :], rope_cos[:, :], ALU.mult)
                        TT(rsw[m][:, :], rsw[m][:, :], rope_sin[:, :], ALU.mult)
                        dve.drain()
                        last = TT(rx[m][:, :], rx[m][:, :], rsw[m][:, :], ALU.add)
                        return last

                    def finish(branch, bank_, weight):
                        dst = yT[:, branch, ds(u, 1), :].rearrange("p a n -> p (a n)")
                        if weight is None:
                            return TT(dst, bank_[:, 0:SEQ], dst, ALU.mult)
                        return STT(dst, bank_[:, 0:SEQ], vec[:, weight:weight + 1], dst, ALU.mult, ALU.mult)

                    dve.wait_ge(sincos_ready, n1)
                    TS(s5_cos, s5_cos, -1.0, 1.0, ALU.mult, ALU.add)
                    dve.drain()
                    invert(1)
                    s5_rotate(0)
                    s5_scan(0)
                    dve.wait_ge(hq_staged, n1)
                    s5_rotate(1)
                    invert(2)
                    s5_scan(1)
                    h_scores(0, None)
                    h_scores(1, None)
                    invert(3)
                    h_scores(2, None)
                    s5_back()
                    h_scores(3, None)
                    invert(4)
                    h_scores(4, None)
                    rope(0)
                    h_scores(5, None)
                    invert(5)
                    h_scores(6, None)
                    h_scores(7, None)
                    rope(1)
                    dve.drain().then_inc(roped, 1)
                    dve.wait_ge(ha_w, ha0 + 9)
                    CP(h_att[:, 1, :], HA[:, 0:P])
                    dve.drain().then_inc(ha_r, 1)
                    invert(6)
                    dve.wait_ge(ra_w, ra0 + 1)
                    TT(r_att[:, 0:2, :].rearrange("p a n -> p (a n)"), RA[:, 0:2 * P],
                       ret_decay[:, ds(u, 1), :].rearrange("p a n -> p (a n)"), ALU.mult)
                    TT(r_att[:, 2, :], RA[:, 2 * P:3 * P],
                       ret_decay[:, ds(u, 1), 0:P].rearrange("p a n -> p (a n)"), ALU.mult)
                    dve.drain().then_inc(ra_r, 1)
                    dve.wait_ge(ga_w, ga0 + 17)
                    CP(vn[:, 0, :], GA[:, 0:P])
                    dve.drain().then_inc(ga_r, 1)
                    dve.wait_ge(sa_w, sa0 + 4)
                    STT(yT[:, 2, ds(u, 1), :].rearrange("p a n -> p (a n)"), s_u[:, :],
                        vec[:, ds(u + V_S5D, 1)], SA[:, 0:SEQ], ALU.mult, ALU.add).then_inc(sa_r, 1)
                    dve.drain().then_inc(s5_used, 1)
                    dve.wait_ge(ga_w, ga0 + 18)
                    STT(vt[:, :], GA[:, 0:P], gfac[:, 5:6], vb[:, 1, :], ALU.mult, ALU.add)
                    dve.drain().then_inc(ga_r, 1)
                    dve.wait_ge(ra_w, ra0 + 2)
                    for a in range(2):
                        nc.vector.bn_stats(r_st[:, a, :], RA[:, a * P:(a + 1) * P])
                    dve.drain()
                    for a in range(2):
                        nc.vector.bn_aggr(r_mv[:, a, :], r_st[:, a, :])
                    dve.drain()
                    TS(r_rs[:, :], r_mv[:, :, 1], EPS, None, ALU.add)
                    dve.drain().then_inc(r_var_ready, 1)
                    dve.wait_ge(ga_w, ga0 + 19)
                    CP(vn[:, 1, :], GA[:, 0:P])
                    dve.drain().then_inc(ga_r, 1)
                    dve.wait_ge(r_rs_ready, n1)
                    for a in range(2):
                        last = TS(r_o[:, a, :], RA[:, a * P:(a + 1) * P], r_mv[:, a, 0:1], r_rs[:, a:a + 1],
                                  ALU.subtract, ALU.mult)
                    dve.drain().then_inc(ra_r, 1)
                    dve.wait_ge(ha_w, ha0 + 11)
                    dve.wait_ge(hz_staged, n1)
                    finish(1, HA, V_HNW).then_inc(ha_r, 1)
                    dve.wait_ge(ra_w, ra0 + 3)
                    dve.wait_ge(rz_staged, n1)
                    finish(3, RA, None).then_inc(ra_r, 1)
                    dve.wait_ge(ga_w, ga0 + 21)
                    dve.wait_ge(gz_staged, n1)
                    finish(0, GA, V_GNW).then_inc(ga_r, 1)
                    dve.drain().then_inc(units_done, 1)

                with dve.Fori(0, GLU_USES) as g:
                    n = dve.snap((l * GLU_USES + g) * TAIL_SLOTS)
                    for i in range(TAIL_SLOTS):
                        v = g * TAIL_SLOTS + i
                        zv = zs[:, ds(v, 1), :].rearrange("p a n -> p (a n)")
                        yv = yT[:, 2, ds(v, 1), :].rearrange("p a n -> p (a n)")
                        dve.wait_ge(glu_sig, n + (i + 3))
                        TT(zv, zv, glu_s[i % 2], ALU.mult)
                        dve.drain()
                        TT(zv, zv, yv, ALU.mult).then_inc(glu_done, 1)
                t0 = dve.snap(l * TAIL_USES)
                with dve.Fori(0, MT) as t:
                    n = dve.snap((l * MT + t) * N_BRANCH)
                    base = dve.snap(t0 + GLU_USES + t * MERGE_USES)
                    mv = merged[:, ds(t, 1), :].rearrange("p a n -> p (a n)")
                    for m in range(N_BRANCH):
                        i = 3 * m + 2
                        dve.wait_ge(tail_used[i % TAIL_SLOTS], base + (i // TAIL_SLOTS + 2))
                        dve.wait_ge(gate_r, n + (m + 3))
                        src = (SA, SB)[m % 2][:, 0:SEQ]
                        if m == 0:
                            TT(mv, src, gate_s[m % 2], ALU.mult)
                        else:
                            TT(prod[:, :], src, gate_s[m % 2], ALU.mult)
                            dve.drain()
                            TT(mv, mv, prod[:, :], ALU.add)
                        dve.drain().then_inc(br_r, 1)
                dve.drain().then_inc(params_used, 1)
                with dve.Fori(0, MT // OUT_TILES) as t:
                    base = dve.snap(t0 + (GLU_USES + MT * MERGE_USES) + t)
                    for i in range(OUT_TILES):
                        dve.wait_ge(tail_used[2 * i + 1], base + 2)
                        xv = xT[:, ds(t * OUT_TILES + i, 1), :].rearrange("p a n -> p (a n)")
                        TT(xv, xv, PJ[i % 2][:, 0:SEQ], ALU.add).then_inc(out_r, 1)
                dve.drain().then_inc(x_ready, 1)
            dve.wait_ge(ms_written, DEPTH + 1)
            mean_square()
            diagonal(DEPTH + 1)
            for k in range(KT):
                last = STT(hT[:, k, :], xT[:, k, :], vec[:, V_FNW + k:V_FNW + k + 1], GA[:, 0:SEQ], ALU.mult, ALU.mult)
            last.then_inc(h_ready, 1)
            for i in range(2 * KT // 4):
                a, k = i // (KT // 4), i % (KT // 4)
                dve.wait_ge(xT_written, KT // 2 + i + 1)
                CP(x_tok[:, a, k * 512:(k + 1) * 512], (GA, GB)[i % 2][:, :]).then_inc(xT_read, 1)

        @block.tensor
        def _(pe):
            def MM(o, w, m, start=True, stop=True):
                return nc.tensor.matmul(o, w, m, start=start, stop=stop)

            TR = nc.tensor.transpose
            pe.wait_ge(consts_in, 16 * 7)
            pe.wait_ge(x_in, 32)
            for k in range(KT // 2):
                if k:
                    pe.wait_ge(xT_read, k)
                for j in range(2):
                    for a in range(2):
                        last = TR(GA[:, j * SEQ + a * P:j * SEQ + (a + 1) * P],
                                  x_tok[:, a, (2 * k + j) * P:(2 * k + j + 1) * P], ident)
                last.then_inc(xT_written, 1)

            def sum_squares(n):
                pe.wait_ge(sq_ready, n)
                for a in range(2):
                    for k in range(KT):
                        last = MM(GA[:, a:a + 1], squares[:, k, a * P:(a + 1) * P], ones[:, 0:1], k == 0, k == KT - 1)
                last.then_inc(ms_written, 1)

            def spread_rms(n):
                pe.wait_ge(diag_ready, n)
                MM(GA[:, 0:SEQ], ones[:, :], am[:, :, :].rearrange("p a n -> p (a n)")).then_inc(rms_spread, 1)

            with pe.Fori(0, DEPTH) as l:
                l1 = pe.snap(l + 1)
                sum_squares(l1)
                pe.wait_ge(params_in, l1 * (16 * 15))
                TR(GB[:, 0:V_ROWS], vec_rows[:, :], ident[0:V_ROWS, 0:V_ROWS]).then_inc(vec_rowsT, 1)
                spread_rms(l1)
                pe.wait_ge(h_ready, l1)
                for a in range(2):
                    for k in range(KT):
                        last = MM(RA[:, a * 2 * UNITS:(a + 1) * 2 * UNITS], hT[:, k, a * P:(a + 1) * P],
                                  w_ab[:, k, :], k == 0, k == KT - 1)
                last.then_inc(ab_written, 1)
                pe.wait_ge(g_ready, l1)
                MM(RA[:, 0:2 * UNITS], upto, gate_g[:, :, :].rearrange("p a u -> p (a u)"))
                MM(RA[:, 2 * UNITS:3 * UNITS], after, gate_g[:, 0, :]).then_inc(gc_written, 1)
                pe.wait_ge(cols_ready, l1)
                pe.wait_ge(s5_rows_ready, l1)
                for a in range(4):
                    last = MM(RA[:, a * STATE_TILES:(a + 1) * STATE_TILES], s5_rows[:, a, :],
                              ident[0:STATE_TILES, 0:STATE_TILES])
                last.then_inc(s5_rowsT, 1)
                t0 = pe.snap(l * TAIL_USES)

                with pe.Fori(0, UNITS) as u:
                    n = pe.snap(l * UNITS + u)
                    n1 = pe.snap(n + 1)
                    pj0, ga0, gb0, ha0 = pe.snap(n * NB), pe.snap(n * GA_N), pe.snap(n * GB_N), pe.snap(n * HA_N)
                    ra0, sa0, cv0 = pe.snap(n * RA_N), pe.snap(n * SA_N), pe.snap(n * 3)
                    w0 = pe.snap(n * (16 * USES))

                    def project(i):
                        s, use, b, h = i % UNIT_SLOTS, i // UNIT_SLOTS, i // 2, i % 2
                        o = PJ[b % 2]
                        if h == 0:
                            pe.wait_ge(pj_read, pj0 + (b + 1))
                        pe.wait_ge(unit_full[s], w0 + 16 * (use + 1))
                        if b in (B_HI, B_RV):
                            first, second = (2 * b) % UNIT_SLOTS, (2 * b + 1) % UNIT_SLOTS
                            pe.wait_ge(unit_full[second], w0 + 16 * ((2 * b + 1) // UNIT_SLOTS + 1))
                            for k in range(KT):
                                w = unit_w[first if k < HALF else second]
                                last = MM(o[:, h * P:(h + 1) * P], hT[:, k, h * P:(h + 1) * P],
                                          w[:, k % HALF, :], k == 0, k == KT - 1)
                                if h == 1 and k == HALF - 1:
                                    last.then_inc(unit_used[first], 1)
                            if h == 1:
                                last.then_inc(unit_used[second], 1)
                            return
                        for k in range(HALF):
                            last = MM(o[:, 0:SEQ], unit_w[s][:, k, :], hT[:, h * HALF + k, :],
                                      h == 0 and k == 0, h == 1 and k == HALF - 1)
                        last.then_inc(unit_used[s], 1)

                    def gdn_bank(stage):
                        pe.wait_ge(ga_r, ga0 + (stage + 1))

                    def g_decay_t():
                        pe.wait_ge(gcols_ready, n1)
                        pe.wait_ge(gb_r, gb0 + 1)
                        MM(GB[:, 0:P], ident, mask_dt, True, False)
                        MM(GB[:, 0:P], g_bc[:, 0, :], upto, False, True)
                        MM(GB[:, P:2 * P], g_bc[:, 1, :], upto)
                        MM(GB[:, 2 * P:3 * P], ident, mask_dt, True, False)
                        MM(GB[:, 2 * P:3 * P], g_bc[:, 1, :], upto, False, True).then_inc(gb_w, 1)

                    def g_decay_s():
                        pe.wait_ge(gb_r, gb0 + 2)
                        for a in range(2):
                            MM(GB[:, a * P:(a + 1) * P], ident, mask_ds, True, False)
                            last = MM(GB[:, a * P:(a + 1) * P], g_bc[:, a, :], neg_upto, False, True)
                        last.then_inc(gb_w, 1)

                    def g_norms():
                        pe.wait_ge(conv_done, cv0 + 2)
                        gdn_bank(0)
                        for m, t in enumerate((gk2, gq2)):
                            for a in range(2):
                                last = MM(GA[:, 2 * m + a:2 * m + a + 1], t[:, a * P:(a + 1) * P], ones[:, 0:1])
                        last.then_inc(ga_w, 1)

                    def g_gram_k():
                        gdn_bank(1)
                        for a in range(2):
                            MM(GA[:, a * P:(a + 1) * P], gk[:, a * P:(a + 1) * P], gk[:, a * P:(a + 1) * P])
                        MM(GA[:, 2 * P:3 * P], gk[:, 0:P], gk[:, P:2 * P]).then_inc(ga_w, 1)

                    def g_values():
                        pe.wait_ge(conv_done, cv0 + 3)
                        pe.wait_ge(gb_r, gb0 + 3)
                        for a in range(2):
                            last = TR(GB[:, a * P:(a + 1) * P], gv[:, a * P:(a + 1) * P], ident)
                        last.then_inc(gb_w, 1)

                    def g_gram_q():
                        gdn_bank(2)
                        MM(GA[:, 0:2 * P], gk[:, 0:P], gq[:, :])
                        MM(GA[:, 2 * P:3 * P], gk[:, P:2 * P], gq[:, P:2 * P]).then_inc(ga_w, 1)

                    def g_first():
                        gdn_bank(3)
                        for a in range(2):
                            last = MM(GA[:, a * P:(a + 1) * P], xm[0][:, a, :], ident)
                        last.then_inc(ga_w, 1)

                    def g_tx(s):
                        gdn_bank(4 + 2 * (s - 1))
                        for a in range(2):
                            last = MM(GA[:, a * P:(a + 1) * P], xm[s % 2][:, a, :], tt[:, 2 + a, :])
                        last.then_inc(ga_w, 1)

                    def g_txt(s):
                        gdn_bank(5 + 2 * (s - 1))
                        for a in range(2):
                            if s + 1 < LEVELS:
                                MM(GA[:, a * P:(a + 1) * P], rr[:, a, :], tt[:, a, :])
                            last = MM(GA[:, (2 + a) * P:(3 + a) * P], tt[:, a, :], rr[:, a, :])
                        last.then_inc(ga_w, 1)

                    def g_new0():
                        gdn_bank(16)
                        MM(GA[:, 0:P], tt[:, 2, :], vb[:, 0, :]).then_inc(ga_w, 1)

                    def g_cross():
                        gdn_bank(17)
                        MM(GA[:, 0:P], kx[:, :], vn[:, 0, :]).then_inc(ga_w, 1)

                    def g_new1():
                        gdn_bank(18)
                        MM(GA[:, 0:P], tt[:, 3, :], vt[:, :]).then_inc(ga_w, 1)

                    def attend(o, att, val):
                        MM(o[:, 0:P], att[:, 0, :], val[:, 0, :])
                        MM(o[:, P:2 * P], att[:, 1, :], val[:, 0, :], True, False)
                        return MM(o[:, P:2 * P], att[:, 2, :], val[:, 1, :], False, True)

                    def to_channels(o, src, used):
                        TR(o[:, 0:P], src[:, 0, :], ident).then_inc(used, 1)
                        return TR(o[:, P:2 * P], src[:, 1, :], ident)

                    def g_out():
                        gdn_bank(19)
                        attend(GA, g_att, vn).then_inc(ga_w, 1)

                    def g_turn():
                        gdn_bank(20)
                        to_channels(GA, g_o, gdn_qkv_used).then_inc(ga_w, 1)

                    def s_turn():
                        pe.wait_ge(bc_padded, n1)
                        pe.wait_ge(sa_r, sa0 + 1)
                        for a in range(4):
                            last = TR(SA[:, a * P:(a + 1) * P], bc_pad[:, a, :], ident)
                        last.then_inc(sa_w, 1)

                    def s_bu(half):
                        pe.wait_ge(u_staged, n1)
                        pe.wait_ge(sa_r, sa0 + (2 + half))
                        for i in range(2):
                            j = 2 * half + i
                            rows_ = slice(32 * j, 32 * j + 32)
                            first = MM(S2[:, i, 0:SEQ], bc_T[rows_, 0, :], s_u[rows_, :])
                            if half == 0 and i == 0:
                                first.then_inc(bc_used, 1)
                            last = MM(S2[:, i, SEQ:2 * SEQ], bc_T[rows_, 1, :], s_u[rows_, :])
                        last.then_inc(sa_w, 1)

                    def s_cx():
                        pe.wait_ge(x_re_im_ready, n1)
                        pe.wait_ge(sa_r, sa0 + 4)
                        for j in range(ST):
                            rows_ = slice(32 * j, 32 * j + 32)
                            MM(SA[rows_, 0:SEQ], bc_T[:, 2, rows_], s5_p[:, j, :], True, False)
                            last = MM(SA[rows_, 0:SEQ], bc_T[:, 3, rows_], s5_q[:, j, :], False, True)
                        last.then_inc(sa_w, 1)

                    def h_pairs(stage):
                        if stage == 0:
                            pe.wait_ge(hq_staged, n1)
                            pe.wait_ge(hsig_used, n1 + 1)
                        pe.wait_ge(ha_r, ha0 + (stage + 1))
                        for a in range(2):
                            last = MM(HA[:, a * P:(a + 1) * P], hk[:, a * P:(a + 1) * P], hq[:, a * P:(a + 1) * P])
                        last.then_inc(ha_w, 1)

                    def h_cross():
                        pe.wait_ge(ha_r, ha0 + 9)
                        MM(HA[:, 0:P], hk[:, 0:P], hq[:, P:2 * P]).then_inc(ha_w, 1)

                    def h_out():
                        pe.wait_ge(hv_staged, n1)
                        pe.wait_ge(ha_r, ha0 + 10)
                        attend(HA, h_att, hv).then_inc(ha_w, 1)

                    def h_turn():
                        pe.wait_ge(ha_r, ha0 + 11)
                        to_channels(HA, h_o, hgrn_used).then_inc(ha_w, 1)

                    def r_scores():
                        pe.wait_ge(roped, n1)
                        pe.wait_ge(ra_r, ra0 + 1)
                        MM(RA[:, 0:2 * P], rx[1][:, 0:P], rx[0][:, :])
                        MM(RA[:, 2 * P:3 * P], rx[1][:, P:2 * P], rx[0][:, P:2 * P]).then_inc(ra_w, 1)

                    def r_out():
                        pe.wait_ge(rv_staged, n1)
                        pe.wait_ge(ra_r, ra0 + 2)
                        attend(RA, r_att, rv).then_inc(ra_w, 1)

                    def r_turn():
                        pe.wait_ge(ra_r, ra0 + 3)
                        to_channels(RA, r_o, ret_used).then_inc(ra_w, 1)

                    project(0)
                    g_decay_t()
                    project(1)
                    g_decay_s()
                    project(2)
                    project(3)
                    project(4)
                    s_turn()
                    project(5)
                    project(6)
                    g_norms()
                    project(7)
                    g_gram_k()
                    project(8)
                    g_values()
                    g_gram_q()
                    project(9)
                    g_first()
                    project(10)
                    g_tx(1)
                    s_bu(0)
                    project(11)
                    g_txt(1)
                    s_bu(1)
                    project(12)
                    g_tx(2)
                    h_pairs(0)
                    project(13)
                    g_txt(2)
                    h_pairs(1)
                    project(14)
                    g_tx(3)
                    h_pairs(2)
                    project(15)
                    g_txt(3)
                    h_pairs(3)
                    project(16)
                    g_tx(4)
                    h_pairs(4)
                    project(17)
                    g_txt(4)
                    h_pairs(5)
                    project(18)
                    g_tx(5)
                    h_pairs(6)
                    project(19)
                    g_txt(5)
                    h_pairs(7)
                    project(20)
                    g_tx(6)
                    h_cross()
                    r_scores()
                    project(21)
                    g_txt(6)
                    h_out()
                    s_cx()
                    project(22)
                    g_new0()
                    r_out()
                    project(23)
                    g_cross()
                    project(24)
                    g_new1()
                    h_turn()
                    project(25)
                    g_out()
                    r_turn()
                    project(26)
                    project(27)
                    g_turn()

                pj_last = pe.snap(l1 * (UNITS * NB) + 2)

                def tail(i, base):
                    pe.wait_ge(tail_full[i % TAIL_SLOTS], base * 16 + 16 * (i // TAIL_SLOTS + 1))
                    return tail_w[i % TAIL_SLOTS]

                with pe.Fori(0, GLU_USES) as g:
                    base = pe.snap(t0 + g)
                    n = pe.snap((l * GLU_USES + g) * TAIL_SLOTS)
                    pe.wait_ge(gelu_done, l1)
                    pe.wait_ge(pj_read, pj_last)
                    for i in range(TAIL_SLOTS):
                        w = tail(i, base)
                        pe.wait_ge(glu_sig, n + (i + 1))
                        for k in range(KB):
                            last = MM(PJ[i % 2][:, 0:SEQ], w[:, k, :], yT[:, 2, k, :], k == 0, k == KB - 1)
                        last.then_inc(tail_used[i], 1)
                units_all = pe.snap(l1 * UNITS)
                t1 = pe.snap(t0 + GLU_USES)
                with pe.Fori(0, MT) as t:
                    base = pe.snap(t1 + t * MERGE_USES)
                    n = pe.snap((l * MT + t) * N_BRANCH)
                    pe.wait_ge(units_done, units_all)
                    pe.wait_ge(glu_sig, units_all + 2)
                    for m, c in enumerate(MERGE_ORDER):
                        pe.wait_ge(gate_r, n + (m + 1))
                        for h in range(2):
                            w = tail(3 * m + h, base)
                            for k in range(HALF):
                                last = MM(PJ[m % 2][:, 0:SEQ], w[:, k, :], hT[:, h * HALF + k, :],
                                          h == 0 and k == 0, h == 1 and k == HALF - 1)
                            last.then_inc(tail_used[(3 * m + h) % TAIL_SLOTS], 1)
                        w = tail(3 * m + 2, base)
                        pe.wait_ge(br_r, n + (m + 1))
                        if c == 2:
                            pe.wait_ge(glu_done, units_all + 2)
                        for k in range(KB):
                            y = zs[:, k, :] if c == 2 else yT[:, c, k, :]
                            last = MM((SA, SB)[m % 2][:, 0:SEQ], w[:, k, :], y, k == 0, k == KB - 1)
                        last.then_inc(tail_used[(3 * m + 2) % TAIL_SLOTS], 1)
                merged_all = pe.snap(l1 * (MT * N_BRANCH) + 2)
                t2 = pe.snap(t1 + MT * MERGE_USES)
                with pe.Fori(0, MT // OUT_TILES) as t:
                    base = pe.snap(t2 + t)
                    pe.wait_ge(br_r, merged_all)
                    n = pe.snap((l * (MT // OUT_TILES) + t) * OUT_TILES)
                    for i in range(OUT_TILES):
                        pe.wait_ge(out_r, n + (i + 1))
                        for h in range(2):
                            w = tail(2 * i + h, base)
                            for k in range(HALF):
                                last = MM(PJ[i % 2][:, 0:SEQ], w[:, k, :], merged[:, h * HALF + k, :],
                                          h == 0 and k == 0, h == 1 and k == HALF - 1)
                            last.then_inc(tail_used[2 * i + h], 1)
                pe.wait_ge(out_r, l1 * MT + 2)
            sum_squares(DEPTH + 1)
            spread_rms(DEPTH + 1)
            pe.wait_ge(h_ready, DEPTH + 1)
            for i in range(2 * KT // 4):
                a, k = i // (KT // 4), i % (KT // 4)
                pe.wait_ge(xT_read, KT // 2 + max(i - 1, 0))
                for j in range(4):
                    last = TR((GA, GB)[i % 2][:, j * P:(j + 1) * P], hT[:, 4 * k + j, a * P:(a + 1) * P], ident)
                last.then_inc(xT_written, 1)


OUT_NAMES = ["out"]


def kernel(**inputs):
    import concourse.bacc as bacc
    from concourse.bass_utils import run_bass_kernel_spmd

    nc = bacc.Bacc("TRN2", target_bir_lowering=False, num_devices=1)
    arrays = {name: np.ascontiguousarray(inputs[name]) for name in INPUTS}
    arrays.update(shape_constants())
    args = {name: nc.dram_tensor(name, a.shape, mybir.dt.from_np(a.dtype), kind="ExternalInput").ap()
            for name, a in arrays.items()}
    out = nc.dram_tensor("out", (1, SEQ, D_MODEL), mybir.dt.float32, kind="ExternalOutput").ap()
    trunk_kernel(nc, args, out)
    got = run_bass_kernel_spmd(nc, [arrays], core_ids=[0])
    return got.results[0]["out"]
```

```python
import math
from contextlib import ExitStack

import numpy as np
import concourse.bass as bass
from concourse import mybir

P = 128
D_MODEL, SEQ, DEPTH = 2048, 256, 2
BRANCH_W = D_MODEL // 2
UNITS = BRANCH_W // P
KT = D_MODEL // P
KB = BRANCH_W // P
EPS = 1e-6
DK_SCALE = float(P) ** -0.5
CONV = 4
S5_GROUP, S5_STATE = 16, 64
S5_GROUPS = BRANCH_W // S5_GROUP
ST = 4
STATE_TILES = ST * UNITS
STATE_ROWS = DEPTH * STATE_TILES
MT = D_MODEL // P
N_BRANCH = 4
SPLIT = (3 * BRANCH_W, UNITS, UNITS, BRANCH_W, BRANCH_W, BRANCH_W, BRANCH_W, BRANCH_W, BRANCH_W, BRANCH_W,
         BRANCH_W, BRANCH_W, BRANCH_W, BRANCH_W, N_BRANCH * D_MODEL)
OFF = [sum(SPLIT[:i]) for i in range(len(SPLIT))]
N_IN = sum(SPLIT)
GQ, GK, GV = 0, BRANCH_W, 2 * BRANCH_W
(GAB, GZ, HQ, HF, HI, HG, SU, SZ, RQ, RK, RV, RG, GATES) = (
    OFF[1], OFF[3], OFF[4], OFF[5], OFF[6], OFF[7], OFF[8], OFF[9], OFF[10], OFF[11], OFF[12], OFF[13], OFF[14])
BLOCKS = (HF, GK, GQ, SU, HQ, GV, HI, RQ, RK, RV, GZ, HG, RG, SZ)
(B_HF, B_GK, B_GQ, B_SU, B_HQ, B_GV, B_HI, B_RQ, B_RK, B_RV, B_GZ, B_HG, B_RG, B_SZ) = range(14)
NB = len(BLOCKS)
HALF = 8
RING = 4
HALVES = 2 * NB
USES = HALVES // RING
MERGE_ORDER = (0, 1, 3, 2)
MERGE_HALVES = 3 * N_BRANCH
MERGE_USES = MERGE_HALVES // RING
OUT_TILES = 2
OUT_PASSES = MT // OUT_TILES
RAW_USES = UNITS * USES + MT * MERGE_USES + OUT_PASSES
SPLITS = RAW_USES * RING
MERGE_SPLIT0 = UNITS * HALVES
OUT_SPLIT0 = MERGE_SPLIT0 + MT * MERGE_HALVES
LEVELS = 7
NEG = -1.0e30
TWO_PI = 2.0 * math.pi
SIN_TURN = 6.283185
MAGIC = 12582912.0
C1, C2 = 6.28125, 1.9352436065673828e-3
C3 = TWO_PI - C1 - C2
V_NORM, V_LB0, V_LB1, V_S5D, V_GLUB, V_GNW, V_HNW, V_FNW = 0, 16, 24, 32, 40, 48, 49, 50
V_ROWS = 66
(C_NGC0, C_SUF0, C_NGC1, C_GC0, C_GC1, C_BETA0, C_BETA1) = range(7)
NCOL = 7
GA_N, GB_N, HA_N, RA_N, SA_N = 20, 4, 11, 5, 4

INPUTS = ['x', 'positions', 'norm_w', 'w_in', 'gdn_conv_w', 'gdn_a_log', 'gdn_dt_bias', 'gdn_norm_w',
          'hgrn_lb_logits', 'hgrn_norm_w', 's5_lambda_re', 's5_lambda_im', 's5_log_dt', 's5_b_re', 's5_b_im',
          's5_c_re', 's5_c_im', 's5_d', 's5_glu_w', 's5_glu_b', 'w_branch', 'w_out', 'final_norm_w']


def shape_constants():
    f = np.float32
    i = np.arange(P)
    row, col = i[:, None], i[None, :]
    squares = np.stack([
        np.eye(P),
        row <= col,
        -1.0 * (row <= col),
        row > col,
        np.where(col >= row, 0.0, NEG),
        np.where(row > col, 0.0, NEG),
    ], axis=1).astype(f)
    lower = np.stack([((row ^ col) >> s == 1) & (row > col) for s in range(LEVELS)], axis=1)
    upper = np.stack([row == col] + [((row ^ col) >> s == 1) & (col > row) for s in range(LEVELS)], axis=1)
    gamma = np.log1p(-np.exp2(-5.0 - np.arange(UNITS)))[None, :, None]
    ahead = (np.arange(SEQ)[None, :] - i[:, None])[:, None, :]
    ret = np.where(ahead >= 0, np.exp(gamma * np.maximum(ahead, 0)) * DK_SCALE, 0.0).astype(f)
    half = P // 2
    inv = (10000.0 ** (-(np.arange(half, dtype=f)) / f(half))).astype(f)
    sign = np.where(i < half, -1.0, 1.0)
    cols = np.zeros((P, 4), f)
    cols[:, 0] = inv[i % half]
    cols[:, 1] = sign
    even = ((i // S5_GROUP) % 2 == 0).astype(f)
    cmask = np.zeros((P, 2, 2, S5_STATE), f)
    for part, s in ((0, 1.0), (1, -1.0)):
        cmask[:, part, 0] = s * even[:, None]
        cmask[:, part, 1] = s * (1 - even)[:, None]
    steps = np.broadcast_to(np.arange(SEQ, dtype=f) - SEQ // 2, (P, SEQ)).copy()
    lsel = np.zeros((P, DEPTH), f)
    lsel[:, 1:] = 1.0
    return {
        "c_squares": squares, "c_masks": np.concatenate([lower, upper], axis=1).astype(f), "c_ret": ret,
        "c_cols": cols, "c_cmask": cmask.reshape(P, 2, 2 * S5_STATE), "c_steps": steps, "c_lsel": lsel,
    }


def trunk_kernel(nc, A, out):
    f32, f32r, u8, i32 = mybir.dt.float32, mybir.dt.float32r, mybir.dt.uint8, mybir.dt.int32
    ALU, ACT = mybir.AluOpType, mybir.ActivationFunctionType
    ds = bass.ds
    ctx = ExitStack()
    with ctx:
        def sb(name, shape, dt=f32):
            return ctx.enter_context(nc.sbuf_tensor(name, shape, dt))

        def bank(name):
            return ctx.enter_context(nc.psum_tensor(name, [P, 512], f32))

        def sem(name):
            return ctx.enter_context(nc.semaphore(name))

        with ExitStack() as again:
            y_parts_a, y_parts_b, y_parts_c = (
                again.enter_context(nc.sbuf_tensor(name, shape, f32r)) for name, shape in (
                    ("y_parts_a", [P, N_BRANCH + 1, UNITS, SEQ]), ("y_parts_b", [P, 2, UNITS, SEQ]),
                    ("y_parts_c", [P, 6 * 4 * SEQ])))
        y_all = sb("y_all", [P, N_BRANCH + 1, UNITS, SEQ])
        yT, zs = y_all[:, 0:N_BRANCH], y_all[:, N_BRANCH]
        work = sb("work", [P, 2 * UNITS * SEQ])
        region = sb("region", [P, 6 * 4 * SEQ])
        xT = sb("xT", [P, KT, SEQ])
        h_hi, h_lo = sb("h_hi", [P, KT, SEQ], f32r), sb("h_lo", [P, KT, SEQ], f32r)
        raw_w = [sb(f"raw_w{s}", [P, HALF, P]) for s in range(RING)]
        w_hi = [sb(f"w_hi{s}", [P, HALF, P], f32r) for s in range(RING)]
        w_lo = [sb(f"w_lo{s}", [P, HALF, P], f32r) for s in range(RING)]
        s5_view = region[:, :].rearrange("p (a t n) -> p a t n", a=6, t=ST)
        s5_cos, s5_sin, s5_re, s5_im, s5_p, s5_q = (s5_view[:, a] for a in range(6))
        merged = region[:, 0:MT * SEQ].rearrange("p (t n) -> p t n", n=SEQ)
        squares = h_full = merged
        h_last = yT[:, 0:2, :, :].rearrange("p c u n -> p (c u) n")
        glu_w = [region[:, 4096 + 1024 * n:5120 + 1024 * n].rearrange("p (k n) -> p k n", n=P) for n in range(2)]
        lam_t = region[0:STATE_ROWS, 4096:5632].rearrange("p (a n) -> p a n", a=12)
        s5_rows = region[0:STATE_ROWS, 5632:6144].rearrange("p (a n) -> p a n", a=4)
        masks_in = region[:, 4096:4096 + (2 * LEVELS + 1) * P].rearrange("p (a n) -> p a n", n=P)
        x_tok = region[:, 0:2 * D_MODEL].rearrange("p (a n) -> p a n", a=2)
        sq = sb("sq", [P, 6, P])
        ident, upto, neg_upto, after, mask_dt, mask_ds = (sq[:, a, :] for a in range(6))
        masks = sb("masks", [P, 2 * LEVELS + 1, P], u8)
        lower, upper = masks[:, 0:LEVELS, :], masks[:, LEVELS:, :]
        ret_decay = sb("ret_decay", [P, SEQ])
        ccols = sb("ccols", [P, 4])
        cmask = sb("cmask", [P, 2, 2 * S5_STATE])
        steps = sb("steps", [P, SEQ])
        lsel = sb("lsel", [P, DEPTH])
        ones = sb("ones", [P, P])
        mhalf = sb("mhalf", [P, 4])
        eps_p = sb("eps_p", [P, 2])
        x_rs = sb("x_rs", [P, 2])
        rope_cos = sb("rope_cos", [P, SEQ])
        rope_sin = sb("rope_sin", [P, SEQ])
        vec_rows = sb("vec_rows", [V_ROWS, P])
        vec = sb("vec", [P, V_ROWS])
        conv_w = sb("conv_w", [P, 3 * UNITS, CONV])
        a_log = sb("a_log", [P, UNITS])
        dt_bias = sb("dt_bias", [P, UNITS])
        w_ab = sb("w_ab", [P, KT, 2 * UNITS])
        ab = sb("ab", [P, 2, 2 * UNITS])
        gate_g = sb("gate_g", [P, 2, UNITS])
        gate_t = sb("gate_t", [P, 4, 2, UNITS])
        unit_cols = sb("unit_cols", [P, UNITS, NCOL])
        lb = sb("lb", [P, UNITS, 2])
        lb_t = sb("lb_t", [P, 4, UNITS])
        lam = sb("lam", [STATE_ROWS, 2, P])
        log_dt = sb("log_dt", [STATE_ROWS, 2])
        s5_par = sb("s5_par", [P, 4, STATE_ROWS + ST])
        work_at = [0]

        def in_work(*shape):
            n0 = work_at[0]
            work_at[0] += math.prod(shape)
            v = work[:, n0:work_at[0]]
            return v if len(shape) == 1 else v.rearrange("p (a n) -> p a n", a=shape[0])

        conv_in = [sb(f"conv_in{n}", [P, CONV - 1 + SEQ]) for n in range(3)]
        gk, gq, gv = (sb(n, [P, SEQ]) for n in ("gk", "gq", "gv"))
        gk2, gq2 = s5_re[:, 0, :], s5_im[:, 0, :]
        gcols = sb("gcols", [P, NCOL])
        g_bc = in_work(2, P)
        dec_t = in_work(3, P)
        dec_s = in_work(2, P)
        gnorm = sb("gnorm", [P, 4])
        gfac = sb("gfac", [P, 12])
        am = sb("am", [P, 2, P])
        kx = in_work(P)
        xm = [in_work(2, P) for n in range(2)]
        tt = in_work(4, P)
        rr = in_work(2, P)
        g_att = in_work(3, P)
        vb = in_work(2, P)
        vn = in_work(2, P)
        vt = in_work(P)
        g_ms = sb("g_ms", [P, 4])
        hsig = in_work(2, SEQ)
        hf = sb("hf", [P, SEQ])
        hq = sb("hq", [P, SEQ])
        hk = sb("hk", [P, SEQ])
        hv = sb("hv", [P, 2, P])
        h_att = sb("h_att", [P, 3, P])
        h_ms = sb("h_ms", [P, 4])
        junk, h_o = (hsig[:, n, :].rearrange("p (a n) -> p a n", a=2) for n in range(2))
        g_o, r_o = xm
        rx = [sb(f"rx{n}", [P, SEQ]) for n in range(2)]
        rsw = [sb(f"rsw{n}", [P, SEQ]) for n in range(2)]
        rv = sb("rv", [P, 2, P])
        r_att = sb("r_att", [P, 3, P])
        r_st = sb("r_st", [P, 2, 6])
        r_mv = sb("r_mv", [P, 2, 2])
        r_rs = sb("r_rs", [P, 2])
        s_u = in_work(SEQ)
        b_raw = sb("b_raw", [P, 2, ST, S5_GROUP])
        c_raw = sb("c_raw", [P, 2, S5_STATE])
        b_t = sb("b_t", [P, 4, ST, S5_GROUP])
        bc_pad = sb("bc_pad", [P, 4, P])
        bc_T = sb("bc_T", [P, 4, P])
        gate_s = [conv_in[n][:, CONV - 1:] for n in range(2)]
        gated = gv
        glu_s = (gk, gq)
        assert work_at[0] == 2 * UNITS * SEQ

        rms = rx[0]

        def y_parts(c):
            hi = (y_parts_b[:, 0], y_parts_b[:, 1], y_parts_a[:, 2],
                  y_parts_c[:, 4096:6144].rearrange("p (u n) -> p u n", u=UNITS))[c]
            return hi, y_parts_a[:, N_BRANCH if c == 2 else c]

        def y_whole(c):
            return zs if c == 2 else yT[:, c]

        PJ = [bank("PJ0"), bank("PJ1")]
        GA, GB, HA, RA = (bank(n) for n in ("GA", "GB", "HA", "RA"))
        S2 = ctx.enter_context(nc.psum_tensor("S2", [P, 2, 512], f32))
        SA, SB = S2[:, 0, :], S2[:, 1, :]

        consts_in, x_in, x_out = sem("consts_in"), sem("x_in"), sem("x_out")
        s5_in, s5_act, s5_dve = sem("s5_in"), sem("s5_act"), sem("s5_dve")
        params_in, params_used = sem("params_in"), sem("params_used")
        raw_full = [sem(f"raw_full{s}") for s in range(RING)]
        raw_used = [sem(f"raw_used{s}") for s in range(RING)]
        hi_ready, split_used = sem("hi_ready"), sem("split_used")
        h_full_ready, h_hi_ready, merged_hi, merged_lo = (
            sem("h_full_ready"), sem("h_hi_ready"), sem("merged_hi"), sem("merged_lo"))
        y_hi_ready, y_lo_ready = sem("y_hi_ready"), sem("y_lo_ready")
        glu_full = [sem(f"glu_full{n}") for n in range(2)]
        glu_used, ret_in = sem("glu_used"), sem("ret_in")
        bc_in, bc_used, bc_padded = sem("bc_in"), sem("bc_used"), sem("bc_padded")
        vec_rowsT, vec_ready = sem("vec_rowsT"), sem("vec_ready")
        s5_rows_ready, s5_rowsT, s5_par_ready = sem("s5_rows_ready"), sem("s5_rowsT"), sem("s5_par_ready")
        xT_written, xT_read = sem("xT_written"), sem("xT_read")
        x_ready = sem("x_ready")
        diag_ready, rms_spread = sem("diag_ready"), sem("rms_spread")
        sq_ready, ms_written, ms_ready, rms_ready, h_ready = (
            sem("sq_ready"), sem("ms_written"), sem("ms_ready"), sem("rms_ready"), sem("h_ready"))
        ab_written, ab_ready, act_p, dve_p = sem("ab_written"), sem("ab_ready"), sem("act_p"), sem("dve_p")
        g_ready, gc_written, cols_ready = sem("g_ready"), sem("gc_written"), sem("cols_ready")
        pj_read = sem("pj_read")
        ga_w, ga_r = sem("ga_written"), sem("ga_read")
        gb_w, gb_r = sem("gb_written"), sem("gb_read")
        ha_w, ha_r = sem("ha_written"), sem("ha_read")
        ra_w, ra_r = sem("ra_written"), sem("ra_read")
        sa_w, sa_r = sem("sa_written"), sem("sa_read")
        gcols_ready = sem("gcols_ready")
        conv_staged, conv_summed, conv_done = sem("conv_staged"), sem("conv_summed"), sem("conv_done")
        gdn_qkv_used = sem("gdn_qkv_used")
        gsum_ready, gnorm_ready = sem("gsum_ready"), sem("gnorm_ready")
        g_ms_ready, g_rs_ready = sem("g_ms_ready"), sem("g_rs_ready")
        h_ms_ready, h_rs_ready = sem("h_ms_ready"), sem("h_rs_ready")
        r_var_ready, r_rs_ready = sem("r_var_ready"), sem("r_rs_ready")
        hsig_staged, hsig_used = sem("hsig_staged"), sem("hsig_used")
        hq_staged, hv_staged, hgrn_used = sem("hq_staged"), sem("hv_staged"), sem("hgrn_used")
        rope_staged, roped, rv_staged, ret_used = (
            sem("rope_staged"), sem("roped"), sem("rv_staged"), sem("ret_used"))
        u_staged, s5_used = sem("u_staged"), sem("s5_used")
        phase_ready, sincos_ready, x_re_im_ready = sem("phase_ready"), sem("sincos_ready"), sem("x_re_im_ready")
        gz_staged, hz_staged, rz_staged = sem("gz_staged"), sem("hz_staged"), sem("rz_staged")
        units_done = sem("units_done")
        gelu_done, glu_sig, glu_done = sem("gelu_done"), sem("glu_sig"), sem("glu_done")
        gate_r, br_r, out_r = sem("gate_read"), sem("branch_read"), sem("out_read")
        rope_ready, rope_done = sem("rope_ready"), sem("rope_done")

        W = A["w_in"].rearrange("l (k p) n -> l p k n", p=P)
        WB = A["w_branch"].rearrange("l c (k p) n -> l c p k n", p=P)
        WO = A["w_out"].rearrange("l (k p) n -> l p k n", p=P)
        WG = A["s5_glu_w"].rearrange("l (k p) n -> l p k n", p=P)
        XV = A["x"].rearrange("b (a p) n -> (b p) a n", p=P)
        OV = out.rearrange("b (a p) n -> (b p) a n", p=P)

        block = ctx.enter_context(nc.Block())

        @block.sync
        def _(sp):
            for name, dst in (("c_squares", sq[:, :, :]), ("c_masks", masks_in), 
                              ("c_cmask", cmask[:, :, :])):
                sp.dma_start(dst, A[name]).then_inc(consts_in, 16)
            for name, dst in (("c_cols", ccols), ("c_steps", steps), ("c_lsel", lsel)):
                sp.dma_start(dst[:, :], A[name]).then_inc(consts_in, 16)
            with sp.Fori(0, DEPTH) as l:
                r0 = sp.snap(l * RAW_USES)

                def load(i, base, source):
                    sp.wait_ge(raw_used[i % RING], base + (i // RING + 1))
                    sp.dma_start(raw_w[i % RING][:, :, :], source.rearrange("l p k n -> (l p) k n")).then_inc(
                        raw_full[i % RING], 16)

                with sp.Fori(0, UNITS) as u:
                    base = sp.snap(r0 + u * USES)
                    for i in range(HALVES):
                        k0 = (i % 2) * HALF
                        load(i, base, W[ds(l, 1), :, k0:k0 + HALF, ds(u * P + BLOCKS[i // 2], P)])
                with sp.Fori(0, MT) as t:
                    base = sp.snap(r0 + UNITS * USES + t * MERGE_USES)
                    for pair in range(2):
                        two = MERGE_ORDER[2 * pair:2 * pair + 2]
                        for j in range(4):
                            load(6 * pair + j, base, W[ds(l, 1), :, (j % 2) * HALF:(j % 2 + 1) * HALF,
                                                       ds(t * P + (GATES + two[j // 2] * D_MODEL), P)])
                        for j in range(2):
                            load(6 * pair + 4 + j, base, WB[ds(l, 1), two[j], :, :, ds(t * P, P)])
                with sp.Fori(0, OUT_PASSES) as t:
                    base = sp.snap(r0 + (UNITS * USES + MT * MERGE_USES) + t)
                    for i in range(RING):
                        h = i % 2
                        load(i, base, WO[ds(l, 1), :, h * HALF:(h + 1) * HALF,
                                         ds(t * (OUT_TILES * P) + (i // 2) * P, P)])
            sp.wait_ge(x_out, 16)

        @block.gpsimd
        def _(pool):
            for s in (pj_read, gate_r, br_r, out_r, glu_sig, glu_done, glu_used):
                pool.sem_inc(s, 2)
            pool.sem_inc(split_used, RING)
            for s in raw_used + [ga_r, gb_r, ha_r, ra_r, sa_r, gdn_qkv_used, hgrn_used, ret_used, s5_used,
                                 bc_used, hsig_used, params_used]:
                pool.sem_inc(s, 1)
            for n, name in enumerate(("s5_lambda_re", "s5_lambda_im")):
                pool.dma_start(lam[:, n, :], A[name].rearrange("l (j g) p -> (l j) (g p)", g=2)).then_inc(s5_in, 16)
            pool.dma_start(log_dt[:, :], A["s5_log_dt"].rearrange("l (j g) -> (l j) g", g=2)).then_inc(s5_in, 16)
            with pool.Fori(0, DEPTH) as l:
                l1 = pool.snap(l + 1)
                pool.wait_ge(params_used, l1)
                rows = [(V_NORM, A["norm_w"][ds(l, 1), :], 16), (V_LB0, A["hgrn_lb_logits"][0:1, :], 8),
                        (V_LB1, A["hgrn_lb_logits"][1:2, :], 8), (V_S5D, A["s5_d"][ds(l, 1), :], 8),
                        (V_GLUB, A["s5_glu_b"][ds(l, 1), :], 8), (V_GNW, A["gdn_norm_w"][ds(l, 1), :], 1),
                        (V_HNW, A["hgrn_norm_w"][ds(l, 1), :], 1)]
                for r, src, n in rows:
                    pool.dma_start(vec_rows[r:r + n, :], src.rearrange("l (t p) -> (l t) p", p=P)).then_inc(
                        params_in, 16)
                pool.dma_start(vec_rows[V_FNW:V_FNW + 16, :],
                               A["final_norm_w"].rearrange("(t p) -> t p", p=P)).then_inc(params_in, 16)
                pool.dma_start(conv_w[:, :, :], A["gdn_conv_w"][ds(l, 1), :, :].rearrange(
                    "l (t p) k -> (l p) t k", p=P)).then_inc(params_in, 16)
                pool.dma_start(a_log[:, :], A["gdn_a_log"][ds(l, 1), :].to_broadcast([P, UNITS])).then_inc(
                    params_in, 16)
                pool.dma_start(dt_bias[:, :], A["gdn_dt_bias"][ds(l, 1), :].to_broadcast([P, UNITS])).then_inc(
                    params_in, 16)
                pool.dma_start(w_ab[:, :, :], W[ds(l, 1), :, :, GAB:GAB + 2 * UNITS].rearrange(
                    "l p k n -> (l p) k n")).then_inc(params_in, 16)

                pool.wait_ge(ms_ready, l1)
                nc.gpsimd.tensor_tensor(x_rs[:, :], x_rs[:, :], mhalf[:, 0:2], ALU.pow).then_inc(rms_ready, 1)
                with pool.Fori(0, UNITS) as u:
                    n1 = pool.snap(l * UNITS + u + 1)
                    pool.wait_ge(bc_used, n1)
                    pool.wait_ge(s5_par_ready, 1)
                    for n, name in enumerate(("s5_b_re", "s5_b_im")):
                        for j in range(ST):
                            pool.dma_start(b_raw[:, n, j, :], A[name][ds(l, 1), ds(u * (2 * ST) + 2 * j, 2), :, :]
                                           .rearrange("l g p c -> (l g p) c")).then_inc(bc_in, 16)
                    for n, name in enumerate(("s5_c_re", "s5_c_im")):
                        pool.dma_start(c_raw[:, n, :], A[name][ds(l, 1), ds(u * (2 * ST), 2 * ST), :, :].rearrange(
                            "l g c p -> (l g c) p")).then_inc(bc_in, 16)
                    pool.wait_ge(bc_in, n1 * (16 * (2 * ST + 2)))
                    scale = [s5_par[:, 2 + n, ds(l * STATE_TILES + u * ST, ST)].unsqueeze(2).to_broadcast([P, ST, S5_GROUP])
                             for n in range(2)]
                    for a, (n, m) in enumerate(((0, 0), (1, 1), (0, 1), (1, 0))):
                        nc.gpsimd.tensor_tensor(b_t[:, a], b_raw[:, n], scale[m], ALU.mult)
                    cview = bc_pad[:, 2:4, :].rearrange("p n (g s) -> p n g s", g=2)
                    for n in range(2):
                        nc.gpsimd.tensor_tensor(
                            cview[:, n], c_raw[:, n, :].unsqueeze(1).to_broadcast([P, 2, S5_STATE]),
                            cmask[:, n, :].rearrange("p (g s) -> p g s", g=2), ALU.mult)
                    pool.drain()
                    bview = bc_pad[:, 0:2, :].rearrange("p n (j g c) -> p n j g c", j=ST, g=2)
                    last = None
                    for g in range(2):
                        rows_g = slice(64 * g, 64 * g + 64)
                        nc.gpsimd.tensor_tensor(bview[rows_g, 0, :, g, :], b_t[rows_g, 0], b_t[rows_g, 1],
                                                ALU.subtract)
                        last = nc.gpsimd.tensor_tensor(bview[rows_g, 1, :, g, :], b_t[rows_g, 2], b_t[rows_g, 3],
                                                       ALU.add)
                    last.then_inc(bc_padded, 1)
                    pool.wait_ge(gsum_ready, n1)
                    nc.gpsimd.tensor_tensor(gnorm[:, :], gnorm[:, :], mhalf[:, 0:4], ALU.pow).then_inc(
                        gnorm_ready, 1)
                    pool.dma_start(ret_decay[:, :], A["c_ret"][:, ds(u, 1), :].rearrange(
                        "p a n -> p (a n)")).then_inc(ret_in, 16)

                    def inverse_root(ms):
                        nc.gpsimd.tensor_tensor(ms[:, 2:4], ms[:, 0:2], eps_p[:, :], ALU.add)
                        pool.drain()
                        nc.gpsimd.tensor_tensor(ms[:, 2:4], ms[:, 2:4], mhalf[:, 0:2], ALU.pow)
                        pool.drain()
                        return nc.gpsimd.tensor_scalar(ms[:, 2:4], ms[:, 2:4], math.sqrt(P), 1.0, ALU.mult, ALU.mult)

                    pool.wait_ge(h_ms_ready, n1)
                    inverse_root(h_ms).then_inc(h_rs_ready, 1)
                    pool.wait_ge(r_var_ready, n1)
                    nc.gpsimd.tensor_tensor(r_rs[:, :], r_rs[:, :], mhalf[:, 0:2], ALU.pow).then_inc(r_rs_ready, 1)
                    pool.wait_ge(g_ms_ready, n1)
                    inverse_root(g_ms)
                    pool.drain()
                    nc.gpsimd.tensor_tensor(g_ms[:, 2:4], g_ms[:, 2:4], gfac[:, 6:8], ALU.mult).then_inc(
                        g_rs_ready, 1)
                with pool.Fori(0, UNITS // 2) as v:
                    n = pool.snap(l * UNITS + v * 2)
                    units_all = pool.snap(l1 * UNITS)
                    pool.wait_ge(units_done, units_all)
                    for i in range(2):
                        pool.wait_ge(glu_used, n + (i + 1))
                        pool.dma_start(glu_w[i], WG[ds(l, 1), :, :, ds(v * (2 * P) + i * P, P)].rearrange(
                            "l p k n -> (l p) k n")).then_inc(glu_full[i], 16)
            pool.wait_ge(ms_ready, DEPTH + 1)
            nc.gpsimd.tensor_tensor(x_rs[:, :], x_rs[:, :], mhalf[:, 0:2], ALU.pow).then_inc(rms_ready, 1)

        @block.scalar
        def _(act):
            A_ = nc.scalar.activation
            act.dma_start(x_tok[:, :, :], XV).then_inc(x_in, 16)
            act.dma_start(hf[:, :].bitcast(i32), A["positions"].to_broadcast([P, SEQ])).then_inc(x_in, 16)
            act.wait_ge(rope_ready, 1)
            A_(rope_sin[:, :], rms[:, :], ACT.Sin, scale=SIN_TURN)
            A_(rope_cos[:, :], rms[:, :], ACT.Sin, scale=SIN_TURN / 2)
            act.drain()
            A_(rope_cos[:, :], rope_cos[:, :], ACT.Square, scale=math.sqrt(2.0))
            act.drain().then_inc(rope_done, 1)
            act.wait_ge(s5_in, 16 * 3)
            A_(log_dt[:, :], log_dt[:, :], ACT.Exp).then_inc(s5_act, 1)
            act.wait_ge(s5_dve, 1)
            A_(s5_rows[:, 0, :], lam_t[:, 0, :], ACT.Exp)
            A_(lam_t[:, 2, :], lam_t[:, 0, :], ACT.Tanh, scale=0.5)
            act.wait_ge(s5_dve, 2)
            A_(lam_t[:, 3, :], s5_rows[:, 1, :], ACT.Sin, scale=SIN_TURN)
            A_(lam_t[:, 4, :], s5_rows[:, 1, :], ACT.Sin, scale=SIN_TURN / 2).then_inc(s5_act, 1)

            def square_x():
                for k in range(0, KT, 4):
                    last = A_(squares[:, k:k + 4, :], xT[:, k:k + 4, :], ACT.Square)
                last.then_inc(sq_ready, 1)

            def split_hi(i, s0, r0):
                act.wait_ge(split_used, s0 + (i + 1))
                act.wait_ge(raw_full[i % RING], r0 * 16 + 16 * (i // RING + 1))
                A_(w_hi[i % RING][:, :, :], raw_w[i % RING][:, :, :], ACT.Copy).then_inc(hi_ready, 1)

            with act.Fori(0, DEPTH) as l:
                l1 = act.snap(l + 1)
                sl, rl = act.snap(l * SPLITS), act.snap(l * RAW_USES)
                act.wait_ge(x_ready, l1)
                square_x()
                for i in range(RING):
                    split_hi(i, sl, rl)
                act.wait_ge(dve_p, l * 2 + 1)
                A_(lb_t[:, 0:2, :], lb_t[:, 0:2, :], ACT.Exp).then_inc(act_p, 1)
                for c in range(4):
                    act.wait_ge(h_full_ready, l * 4 + (c + 1))
                    A_(h_hi[:, 4 * c:4 * c + 4, :], h_full[:, 4 * c:4 * c + 4, :], ACT.Copy).then_inc(h_hi_ready, 1)
                act.wait_ge(dve_p, l * 2 + 2)
                A_(gate_t[:, 0], ab[:, :, 0:UNITS], ACT.Exp, scale=-1.0)
                A_(gate_t[:, 2], gate_t[:, 2], ACT.Exp, scale=-1.0)
                A_(a_log[:, :], a_log[:, :], ACT.Exp)
                act.drain()
                A_(gate_t[:, 2], gate_t[:, 2], ACT.Ln, bias=1.0).then_inc(act_p, 1)

                with act.Fori(0, UNITS) as u:
                    n = act.snap(l * UNITS + u)
                    n1 = act.snap(n + 1)
                    s0, r0 = act.snap(sl + u * HALVES), act.snap(rl + u * USES)
                    ga0, gb0 = act.snap(n * GA_N), act.snap(n * GB_N)
                    ha0, sa0, cv0 = act.snap(n * HA_N), act.snap(n * SA_N), act.snap(n * 3)

                    def projected(b):
                        act.wait_ge(split_used, s0 + (2 * b + 2 + RING))
                        return PJ[b % 2][:, 0:SEQ]

                    def ahead(i):
                        split_hi(i + RING, s0, r0)

                    def decays_t():
                        act.wait_ge(gb_w, gb0 + 1)
                        for a, c in enumerate((C_NGC0, C_SUF0, C_NGC1)):
                            last = A_(dec_t[:, a, :], GB[:, a * P:(a + 1) * P], ACT.Exp, bias=gcols[:, c:c + 1])
                        last.then_inc(gb_r, 1)

                    def decays_s():
                        act.wait_ge(gb_w, gb0 + 2)
                        for a, c in enumerate((C_GC0, C_GC1)):
                            last = A_(dec_s[:, a, :], GB[:, a * P:(a + 1) * P], ACT.Exp, bias=gcols[:, c:c + 1])
                        last.then_inc(gb_r, 1)

                    def stage_conv(b, m):
                        src = projected(b)
                        A_(conv_in[m][:, CONV - 1:], src, ACT.Copy)
                        A_((gk, gq, gv)[m][:, :], src, ACT.Copy, scale=tap(m, CONV - 1)).then_inc(pj_read, 1)

                    def tap(m, k):
                        part = (1, 0, 2)[m]
                        return conv_w[:, ds(u + part * UNITS, 1), k:k + 1].rearrange("p a b -> p (a b)")

                    def silu_conv(m, square=None):
                        act.wait_ge(conv_summed, cv0 + (m + 1))
                        t = (gk, gq, gv)[m]
                        last = A_(t[:, :], t[:, :], ACT.Silu)
                        if square is not None:
                            act.drain()
                            last = A_(square, t[:, :], ACT.Square)
                        last.then_inc(conv_done, 1)

                    def square_sums(src, ms, scale):
                        for a in range(2):
                            last = A_(junk[:, a, :], src[:, a * P:(a + 1) * P], ACT.Square,
                                      scale=scale[a], accum_out=ms[:, a:a + 1])
                        return last

                    def gate_of(branch):
                        return yT[:, branch, ds(u, 1), :].rearrange("p a n -> p (a n)")

                    def copy_r(s):
                        act.wait_ge(ga_w, ga0 + (4 + 2 * (s - 1)))
                        A_(rr[:, :, :], GA[:, 0:2 * P], ACT.Copy).then_inc(ga_r, 1)

                    def values_back(val, staged, stage):
                        act.wait_ge(ra_w, n * RA_N + stage)
                        A_(val[:, :, :], RA[:, 0:2 * P], ACT.Copy).then_inc(ra_r, 1)
                        act.drain().then_inc(staged, 1)

                    def stage_rope(m, b):
                        src = projected(b)
                        A_(rx[m][:, :], src, ACT.Copy)
                        A_(rsw[m][0:64, :], src[64:128, :], ACT.Copy)
                        A_(rsw[m][64:128, :], src[0:64, :], ACT.Copy).then_inc(pj_read, 1)
                        act.drain().then_inc(rope_staged, 1)

                    ahead(0)
                    act.wait_ge(gcols_ready, n1)
                    act.wait_ge(gdn_qkv_used, n1)
                    decays_t()
                    act.wait_ge(hsig_used, n1)
                    src = projected(B_HF)
                    A_(hsig[:, 0, :], src, ACT.Exp, scale=-1.0)
                    A_(hsig[:, 1, :], src, ACT.Exp).then_inc(pj_read, 1)
                    act.drain().then_inc(hsig_staged, 1)
                    ahead(1)
                    decays_s()
                    act.wait_ge(phase_ready, l + n1)
                    A_(s5_sin, s5_p, ACT.Sin, scale=SIN_TURN)
                    A_(s5_cos, s5_p, ACT.Sin, scale=SIN_TURN / 2)
                    ahead(2)
                    stage_conv(B_GK, 0)
                    act.drain().then_inc(conv_staged, 1)
                    ahead(3)
                    A_(s5_cos, s5_cos, ACT.Square, scale=math.sqrt(2.0))
                    act.wait_ge(sa_w, sa0 + 1)
                    A_(bc_T[:, :, :], SA, ACT.Copy).then_inc(sa_r, 1)
                    silu_conv(0, gk2)
                    ahead(4)
                    stage_conv(B_GQ, 1)
                    act.drain().then_inc(conv_staged, 1)
                    ahead(5)
                    silu_conv(1, gq2)
                    ahead(6)
                    A_(s5_cos, s5_cos, ACT.Copy, scale=-1.0, bias=1.0).then_inc(sincos_ready, 1)
                    act.wait_ge(s5_used, n1)
                    A_(s_u[:, :], projected(B_SU), ACT.Copy).then_inc(pj_read, 1)
                    act.drain().then_inc(u_staged, 1)
                    ahead(7)
                    ahead(8)
                    act.wait_ge(hgrn_used, n1)
                    A_(hq[:, :], projected(B_HQ), ACT.Silu).then_inc(pj_read, 1)
                    act.drain().then_inc(hq_staged, 1)
                    ahead(9)
                    copy_r(1)
                    ahead(10)
                    stage_conv(B_GV, 2)
                    act.drain().then_inc(conv_staged, 1)
                    ahead(11)
                    copy_r(2)
                    ahead(12)
                    A_(hv[:, :, :], projected(B_HI), ACT.Copy).then_inc(pj_read, 1)
                    act.drain().then_inc(hv_staged, 1)
                    ahead(13)
                    copy_r(3)
                    values_back(hv, hv_staged, 1)
                    ahead(14)
                    act.wait_ge(ret_used, n1)
                    stage_rope(0, B_RQ)
                    ahead(15)
                    copy_r(4)
                    ahead(16)
                    stage_rope(1, B_RK)
                    ahead(17)
                    copy_r(5)
                    silu_conv(2)
                    ahead(18)
                    A_(rv[:, :, :], projected(B_RV), ACT.Copy).then_inc(pj_read, 1)
                    act.drain().then_inc(rv_staged, 1)
                    ahead(19)
                    copy_r(6)
                    ahead(20)
                    act.wait_ge(ha_w, ha0 + 10)
                    square_sums(HA, h_ms, (1.0, 1.0))
                    act.drain().then_inc(h_ms_ready, 1)
                    A_(gate_of(0), projected(B_GZ), ACT.Silu).then_inc(pj_read, 1)
                    act.drain().then_inc(gz_staged, 1)
                    ahead(21)
                    values_back(rv, rv_staged, 3)
                    ahead(22)
                    act.wait_ge(h_rs_ready, n1)
                    for a in range(2):
                        last = A_(h_o[:, a, :], HA[:, a * P:(a + 1) * P], ACT.Copy, scale=h_ms[:, 2 + a:3 + a])
                    last.then_inc(ha_r, 1)
                    A_(gate_of(1), projected(B_HG), ACT.Silu).then_inc(pj_read, 1)
                    act.drain().then_inc(hz_staged, 1)
                    ahead(23)
                    ahead(24)
                    act.wait_ge(ga_w, ga0 + 19)
                    square_sums(GA, g_ms, (gfac[:, 6:7], gfac[:, 7:8]))
                    act.drain().then_inc(g_ms_ready, 1)
                    A_(gate_of(3), projected(B_RG), ACT.Silu).then_inc(pj_read, 1)
                    act.drain().then_inc(rz_staged, 1)
                    ahead(25)
                    act.wait_ge(g_rs_ready, n1)
                    for a in range(2):
                        last = A_(g_o[:, a, :], GA[:, a * P:(a + 1) * P], ACT.Copy, scale=g_ms[:, 2 + a:3 + a])
                    last.then_inc(ga_r, 1)
                    ahead(26)
                    A_(zs[:, ds(u, 1), :].rearrange("p a n -> p (a n)"), projected(B_SZ), ACT.Silu).then_inc(
                        pj_read, 1)
                    ahead(27)

                act.wait_ge(units_done, l1 * UNITS)
                for k in range(0, UNITS, 4):
                    last = A_(yT[:, 2, k:k + 4, :], yT[:, 2, k:k + 4, :], ACT.Gelu_apprx_tanh)
                last.then_inc(gelu_done, 1)

                def y_high(m):
                    hi = y_parts(MERGE_ORDER[m])[0]
                    src = y_whole(MERGE_ORDER[m])
                    for k in range(0, UNITS, 4):
                        last = A_(hi[:, k:k + 4, :], src[:, k:k + 4, :], ACT.Copy)
                    last.then_inc(y_hi_ready, 1)

                y_high(0)
                y_high(1)
                with act.Fori(0, UNITS // 2) as v:
                    n = act.snap(l * UNITS + v * 2)
                    for i in range(2):
                        act.wait_ge(glu_used, n + (i + 3))
                        act.wait_ge(glu_done, n + (i + 1))
                        A_(glu_s[i][:, :], PJ[i][:, 0:SEQ], ACT.Sigmoid,
                           bias=vec[:, ds(v * 2 + (V_GLUB + i), 1)]).then_inc(glu_sig, 1)
                act.wait_ge(glu_done, l1 * UNITS + 2)
                y_high(2)
                y_high(3)
                with act.Fori(0, MT) as t:
                    n = act.snap((l * MT + t) * N_BRANCH)
                    s0 = act.snap(sl + MERGE_SPLIT0 + t * MERGE_HALVES)
                    r0 = act.snap(rl + UNITS * USES + t * MERGE_USES)
                    for pair in range(2):
                        for m in (2 * pair, 2 * pair + 1):
                            for h in range(2):
                                i = 6 * pair + 2 * (m % 2) + h
                                split_hi(i + RING, s0, r0)
                            act.wait_ge(br_r, n + (m + 1))
                            A_(gate_s[m % 2], PJ[m % 2][:, 0:SEQ], ACT.Sigmoid).then_inc(gate_r, 1)
                        for i in (6 * pair + 4, 6 * pair + 5):
                            split_hi(i + RING, s0, r0)
                act.wait_ge(br_r, l1 * (MT * N_BRANCH) + 2)
                for c in range(4):
                    A_(h_hi[:, 4 * c:4 * c + 4, :], merged[:, 4 * c:4 * c + 4, :], ACT.Copy).then_inc(merged_hi, 1)
                with act.Fori(0, OUT_PASSES - 1) as t:
                    s0 = act.snap(sl + OUT_SPLIT0 + t * RING)
                    r0 = act.snap(rl + (UNITS * USES + MT * MERGE_USES) + t)
                    for i in range(RING):
                        split_hi(i + RING, s0, r0)
            act.wait_ge(x_ready, DEPTH + 1)
            square_x()
            act.wait_ge(xT_read, KT // 2 + 2 * KT // 4)
            act.dma_start(OV, x_tok).then_inc(x_out, 16)

        @block.vector
        def _(dve):
            TS, TT, STT = nc.vector.tensor_scalar, nc.vector.tensor_tensor, nc.vector.scalar_tensor_tensor
            CP = nc.vector.tensor_copy

            for n in range(3):
                nc.vector.memset(conv_in[n][:, 0:CONV - 1], 0.0)
            nc.vector.memset(h_att[:, :, :], 0.0)
            nc.vector.memset(bc_pad[:, :, :], 0.0)
            nc.vector.memset(ones[:, :], 1.0)
            nc.vector.memset(s5_par[:, :, STATE_ROWS:], 0.0)
            nc.vector.memset(mhalf[:, :], -0.5)
            nc.vector.memset(eps_p[:, :], EPS * P)
            pos_i = hf[:, :].bitcast(i32)
            dve.wait_ge(x_in, 32)
            CP(hq[:, :], pos_i)
            dve.wait_ge(consts_in, 16 * 6)
            CP(masks[:, :, :], masks_in)
            dve.drain()

            def reduce_turns(dst, angle, n_buf):
                TS(n_buf, angle, 1.0 / TWO_PI, MAGIC, ALU.mult, ALU.add)
                dve.drain()
                TS(n_buf, n_buf, MAGIC, None, ALU.subtract)
                dve.drain()
                for c in (C1, C2, C3):
                    STT(angle, n_buf, -c, angle, ALU.mult, ALU.add)
                    dve.drain()
                TS(dst, angle, 1.0 / TWO_PI, 0.5, ALU.mult, ALU.min)
                dve.drain()
                return TS(dst, dst, -0.5, None, ALU.max)

            TS(hq[:, :], hq[:, :], ccols[:, 0:1], None, ALU.mult)
            dve.drain()
            reduce_turns(rms[:, :], hq[:, :], hk[:, :]).then_inc(rope_ready, 1)
            dve.wait_ge(rope_done, 1)
            TS(rope_cos[:, :], rope_cos[:, :], -1.0, 1.0, ALU.mult, ALU.add)
            TS(rope_sin[:, :], rope_sin[:, :], ccols[:, 1:2], None, ALU.mult)
            L = lambda a: lam_t[:, a, :]
            dve.wait_ge(s5_act, 1)
            dtb = log_dt[:, :].unsqueeze(2).to_broadcast([STATE_ROWS, 2, S5_STATE])
            v3 = lambda ap: ap.rearrange("p (g s) -> p g s", g=2)
            TT(v3(L(0)), v3(lam[:, 0, :]), dtb, ALU.mult)
            TT(v3(L(1)), v3(lam[:, 1, :]), dtb, ALU.mult)
            dve.drain().then_inc(s5_dve, 1)
            reduce_turns(s5_rows[:, 1, :], L(1), L(5))
            dve.drain().then_inc(s5_dve, 1)
            for k in range(KT // 2):
                dve.wait_ge(xT_written, k + 1)
                CP(xT[:, 2 * k:2 * k + 2, :], (GA, GB)[k % 2].rearrange("p (a n) -> p a n", a=2)).then_inc(xT_read, 1)
            dve.drain().then_inc(x_ready, 1)
            dve.wait_ge(s5_act, 2)
            TS(L(2), L(2), 0.5, None, ALU.min)
            TT(L(5), L(4), L(4), ALU.mult)
            TS(L(6), L(0), 0.5, None, ALU.is_gt)
            TS(L(7), s5_rows[:, 0, :], -1.0, None, ALU.add)
            TT(L(10), lam[:, 0, :], lam[:, 0, :], ALU.mult)
            TT(L(11), lam[:, 1, :], lam[:, 1, :], ALU.mult)
            dve.drain()
            TS(L(8), L(2), -1.0, 1.0, ALU.mult, ALU.add)
            TS(L(5), L(5), -2.0, None, ALU.mult)
            TT(L(10), L(10), L(11), ALU.add)
            dve.drain()
            nc.vector.reciprocal(L(8), L(8))
            nc.vector.reciprocal(L(10), L(10))
            dve.drain()
            STT(L(8), L(2), 2.0, L(8), ALU.mult, ALU.mult)
            dve.drain()
            TT(L(7), L(7), L(8), ALU.subtract)
            dve.drain()
            TT(L(7), L(7), L(6), ALU.mult)
            dve.drain()
            TT(L(8), L(8), L(7), ALU.add)
            TS(L(9), L(5), 1.0, None, ALU.add)
            TT(L(3), L(3), s5_rows[:, 0, :], ALU.mult)
            dve.drain()
            TT(L(8), L(8), L(9), ALU.mult)
            dve.drain()
            TT(L(8), L(8), L(5), ALU.add)
            dve.drain()
            TT(L(5), L(8), lam[:, 0, :], ALU.mult)
            TT(L(6), L(3), lam[:, 1, :], ALU.mult)
            TT(L(7), L(3), lam[:, 0, :], ALU.mult)
            TT(L(9), L(8), lam[:, 1, :], ALU.mult)
            dve.drain()
            TT(L(5), L(5), L(6), ALU.add)
            TT(L(7), L(7), L(9), ALU.subtract)
            dve.drain()
            TT(s5_rows[:, 2, :], L(5), L(10), ALU.mult)
            TT(s5_rows[:, 3, :], L(7), L(10), ALU.mult)
            dve.drain().then_inc(s5_rows_ready, 1)
            dve.wait_ge(s5_rowsT, 1)
            CP(s5_par[:, :, 0:STATE_ROWS], RA[:, 0:4 * STATE_ROWS].rearrange("p (a n) -> p a n", a=4))
            dve.drain().then_inc(s5_par_ready, 1)

            def mean_square():
                TS(x_rs[:, :], GA[:, 0:2], 1.0 / D_MODEL, EPS, ALU.mult, ALU.add).then_inc(ms_ready, 1)

            def diagonal(n):
                dve.wait_ge(rms_ready, n)
                for a in range(2):
                    TS(am[:, a, :], ident, x_rs[:, a:a + 1], None, ALU.mult)
                dve.drain().then_inc(diag_ready, 1)
                dve.wait_ge(rms_spread, n)

            def split_lo(i, s0):
                dve.wait_ge(hi_ready, s0 + (i + 1))
                TT(w_lo[i % RING][:, :, :], raw_w[i % RING][:, :, :], w_hi[i % RING][:, :, :].bitcast(f32),
                   ALU.subtract).then_inc(raw_used[i % RING], 1)

            def low_part(c, full):
                k = slice(4 * c, 4 * c + 4)
                return TT(h_lo[:, k, :], full[:, k, :], h_hi[:, k, :].bitcast(f32), ALU.subtract)

            with dve.Fori(0, DEPTH) as l:
                l1 = dve.snap(l + 1)
                a0 = dve.snap(l * 2)
                sl = dve.snap(l * SPLITS)
                dve.wait_ge(vec_rowsT, l1)
                CP(vec[:, :], GB[:, 0:V_ROWS]).then_inc(vec_ready, 1)
                dve.drain()
                V0, V1 = vec[:, V_LB0:V_LB0 + UNITS], vec[:, V_LB1:V_LB1 + UNITS]
                TT(lb_t[:, 2, :], V0, V1, ALU.max)
                dve.drain()
                TT(lb_t[:, 0, :], V0, lb_t[:, 2, :], ALU.subtract)
                TT(lb_t[:, 1, :], V1, lb_t[:, 2, :], ALU.subtract).then_inc(dve_p, 1)
                def s5_phases(*tiles):
                    for j, tile in enumerate(tiles):
                        TS(s5_p[:, j, :], steps[:, :], s5_par[:, 1, tile], None, ALU.mult)
                    dve.drain()
                    TS(s5_q, s5_p, MAGIC, MAGIC, ALU.add, ALU.subtract)
                    dve.drain()
                    TT(s5_p, s5_p, s5_q, ALU.subtract).then_inc(phase_ready, 1)

                s5_phases(*(ds(l * STATE_TILES + j, 1) for j in range(ST)))
                for i in range(RING):
                    split_lo(i, sl)
                dve.wait_ge(ms_written, l1)
                mean_square()
                diagonal(l1)
                for k in range(KT):
                    last = STT(h_full[:, k, :], xT[:, k, :], vec[:, V_NORM + k:V_NORM + k + 1], GA[:, 0:SEQ],
                               ALU.mult, ALU.mult)
                    if k % 4 == 3:
                        last.then_inc(h_full_ready, 1)
                for c in range(4):
                    dve.wait_ge(h_hi_ready, l * 4 + (c + 1))
                    low_part(c, h_full).then_inc(h_ready, 1)
                dve.wait_ge(ab_written, l1)
                CP(ab[:, :, :], RA[:, 0:4 * UNITS].rearrange("p (a n) -> p a n", a=2))
                dve.drain()
                TT(gate_t[:, 1], ab[:, :, UNITS:2 * UNITS],
                   dt_bias[:, :].unsqueeze(1).to_broadcast([P, 2, UNITS]), ALU.add)
                dve.drain()
                TS(gate_t[:, 3], gate_t[:, 1], 0.0, None, ALU.max)
                STT(gate_t[:, 2], gate_t[:, 1], -1.0, gate_t[:, 1], ALU.mult, ALU.max)
                dve.drain().then_inc(dve_p, 1)
                dve.wait_ge(act_p, a0 + 1)
                TT(lb_t[:, 2, :], lb_t[:, 0, :], lb_t[:, 1, :], ALU.add)
                dve.drain()
                nc.vector.reciprocal(lb_t[:, 2, :], lb_t[:, 2, :])
                dve.drain()
                TT(lb_t[:, 0, :], lb_t[:, 0, :], lb_t[:, 2, :], ALU.mult)
                TT(lb_t[:, 1, :], lb_t[:, 1, :], lb_t[:, 2, :], ALU.mult)
                dve.drain()
                STT(lb_t[:, 1, :], lb_t[:, 1, :], lsel[:, ds(l, 1)], lb_t[:, 0, :], ALU.mult, ALU.add)
                dve.drain()
                TT(lb[:, :, 0], lb_t[:, 1, :], lb_t[:, 0, :], ALU.subtract)
                dve.drain()
                TS(lb[:, :, 1], lb[:, :, 0], -1.0, 1.0, ALU.mult, ALU.add)
                dve.wait_ge(act_p, a0 + 2)
                TS(gate_t[:, 0], gate_t[:, 0], 1.0, None, ALU.add)
                TT(gate_t[:, 3], gate_t[:, 3], gate_t[:, 2], ALU.add)
                dve.drain()
                beta_out = unit_cols[:, :, C_BETA0:C_BETA1 + 1].rearrange("p u a -> p a u")
                nc.vector.reciprocal(beta_out, gate_t[:, 0])
                STT(gate_g[:, :, :], gate_t[:, 3], -1.0, a_log[:, :].unsqueeze(1).to_broadcast([P, 2, UNITS]),
                    ALU.mult, ALU.mult).then_inc(g_ready, 1)
                dve.wait_ge(gc_written, l1)
                G16 = RA[:, 0:2 * UNITS].rearrange("p (a u) -> p u a", a=2)
                TS(unit_cols[:, :, C_GC0:C_GC1 + 1], G16, 1.0, None, ALU.mult)
                TS(unit_cols[:, :, C_NGC0:C_NGC1 + 1:2], G16, -1.0, None, ALU.mult)
                TS(unit_cols[:, :, C_SUF0], RA[:, 2 * UNITS:3 * UNITS], 1.0, None, ALU.mult)
                dve.drain().then_inc(cols_ready, 1)
                with dve.Fori(0, UNITS) as u:
                    n = dve.snap(l * UNITS + u)
                    n1 = dve.snap(n + 1)
                    ga0, gb0, ha0 = dve.snap(n * GA_N), dve.snap(n * GB_N), dve.snap(n * HA_N)
                    ra0, sa0, cv0 = dve.snap(n * RA_N), dve.snap(n * SA_N), dve.snap(n * 3)

                    def tap(m, k):
                        part = (1, 0, 2)[m]
                        return conv_w[:, ds(u + part * UNITS, 1), k:k + 1].rearrange("p a b -> p (a b)")

                    def conv_taps(m):
                        dve.wait_ge(conv_staged, cv0 + (m + 1))
                        t = (gk, gq, gv)[m]
                        for k in range(CONV - 2, -1, -1):
                            last = STT(t[:, :], conv_in[m][:, k:k + SEQ], tap(m, k), t[:, :], ALU.mult, ALU.add)
                            if k:
                                dve.drain()
                        last.then_inc(conv_summed, 1)

                    s0 = dve.snap(sl + u * HALVES)

                    def ahead(i):
                        split_lo(i + RING, s0)

                    def level_mask(s, dst):
                        TT(dst[:, :, :], am[:, :, :], lower[:, s, :].unsqueeze(1).to_broadcast([P, 2, P]), ALU.mult)

                    def invert(s):
                        if s + 1 < LEVELS:
                            level_mask(s + 1, xm[(s + 1) % 2])
                        dve.wait_ge(ga_w, ga0 + (5 + 2 * (s - 1)))
                        first = 0 if s + 1 < LEVELS else 2
                        TT(tt[:, first:4, :].rearrange("p a n -> p (a n)"),
                           tt[:, first:4, :].rearrange("p a n -> p (a n)"), GA[:, first * P:4 * P], ALU.subtract)
                        dve.drain().then_inc(ga_r, 1)

                    def s5_turn(half):
                        j = slice(2 * half, 2 * half + 2)
                        re, im = S2[:, :, 0:SEQ], S2[:, :, SEQ:2 * SEQ]
                        dve.wait_ge(sa_w, sa0 + (2 + half))
                        TT(s5_p[:, 0:2], re, s5_cos[:, j], ALU.mult)
                        TT(s5_q[:, 0:2], im, s5_sin[:, j], ALU.mult)
                        TT(s5_p[:, 2:4], im, s5_cos[:, j], ALU.mult)
                        TT(s5_q[:, 2:4], re, s5_sin[:, j], ALU.mult).then_inc(sa_r, 1)
                        dve.drain()

                    def s5_add(half):
                        j = slice(2 * half, 2 * half + 2)
                        TT(s5_re[:, j], s5_p[:, 0:2], s5_q[:, 0:2], ALU.add)
                        TT(s5_im[:, j], s5_p[:, 2:4], s5_q[:, 2:4], ALU.subtract)
                        dve.drain()

                    def s5_scan(half):
                        for j in range(2 * half, 2 * half + 2):
                            mag = s5_par[:, 0, ds(l * STATE_TILES + u * ST + j, 1)].to_broadcast([P, SEQ])
                            for v in (s5_re, s5_im):
                                nc.vector.tensor_tensor_scan(v[:, j, :], mag, v[:, j, :], 0.0, ALU.mult, ALU.add)

                    def s5_back(step):
                        dve.drain()
                        a, b, c, op = ((s5_p, s5_re, s5_cos, ALU.mult), (s5_q, s5_im, s5_sin, ALU.mult),
                                       (s5_p, s5_p, s5_q, ALU.subtract), (s5_re, s5_re, s5_sin, ALU.mult),
                                       (s5_im, s5_im, s5_cos, ALU.mult), (s5_q, s5_im, s5_re, ALU.add))[step]
                        TT(a, b, c, op)
                        if step == 5:
                            dve.drain().then_inc(x_re_im_ready, 1)

                    def h_scores(stage):
                        dve.wait_ge(ha_w, ha0 + (stage + 1))
                        if stage == 0:
                            TT(hq[:, :], hq[:, :], hf[:, :], ALU.mult)
                        else:
                            s = 1 << (stage - 1)
                            tot = hf[:, 0:SEQ:s].rearrange("p (b two) -> p b two", two=2)
                            nblk = SEQ // (2 * s)
                            q2 = hq[:, :].rearrange("p (b two s) -> p b two s", two=2, s=s)[:, :, 1, :]
                            k2 = hk[:, :].rearrange("p (b two s) -> p b two s", two=2, s=s)[:, :, 0, :]
                            TT(q2, q2, tot[:, :, 0:1].to_broadcast([P, nblk, s]), ALU.mult)
                            TT(k2, k2, tot[:, :, 1:2].to_broadcast([P, nblk, s]), ALU.mult)
                            dve.drain()
                            TT(hf[:, 0:SEQ:2 * s], tot[:, :, 0], tot[:, :, 1], ALU.mult)
                        nc.vector.copy_predicated(
                            h_att[:, 0:3:2, :], upper[:, stage, :].unsqueeze(1).to_broadcast([P, 2, P]),
                            HA[:, 0:2 * P].rearrange("p (a n) -> p a n", a=2))
                        dve.drain().then_inc(ha_r, 1)

                    def rope(m):
                        dve.wait_ge(rope_staged, n * 2 + (m + 1))
                        TT(rx[m][:, :], rx[m][:, :], rope_cos[:, :], ALU.mult)
                        TT(rsw[m][:, :], rsw[m][:, :], rope_sin[:, :], ALU.mult)
                        dve.drain()
                        last = TT(rx[m][:, :], rx[m][:, :], rsw[m][:, :], ALU.add)
                        return last

                    def finish(branch, bank_, weight):
                        dst = yT[:, branch, ds(u, 1), :].rearrange("p a n -> p (a n)")
                        if weight is None:
                            return TT(dst, bank_[:, 0:SEQ], dst, ALU.mult)
                        return STT(dst, bank_[:, 0:SEQ], vec[:, weight:weight + 1], dst, ALU.mult, ALU.mult)

                    dve.wait_ge(gdn_qkv_used, n1)
                    CP(gcols[:, :], unit_cols[:, ds(u, 1), :].rearrange("p a c -> p (a c)"))
                    for a in range(2):
                        CP(g_bc[:, a, :], gate_g[:, a, ds(u, 1)].to_broadcast([P, P]))
                    dve.drain().then_inc(gcols_ready, 1)
                    ahead(0)
                    ahead(1)
                    dve.wait_ge(hsig_staged, n1)
                    TS(hsig[:, :, :], hsig[:, :, :], 1.0, None, ALU.add)
                    dve.drain()
                    nc.vector.reciprocal(hsig[:, 0, :], hsig[:, 0, :])
                    ahead(2)
                    conv_taps(0)
                    ahead(3)
                    ahead(4)
                    conv_taps(1)
                    ahead(5)
                    ahead(6)
                    dve.wait_ge(gb_w, gb0 + 3)
                    TS(gnorm[:, :], GB[:, 0:4], EPS, None, ALU.add).then_inc(gb_r, 1)
                    dve.drain().then_inc(gsum_ready, 1)
                    dve.wait_ge(gnorm_ready, n1)
                    TT(gfac[:, 0:2], gnorm[:, 0:2], gcols[:, C_BETA0:C_BETA1 + 1], ALU.mult)
                    TS(gfac[:, 6:8], gnorm[:, 2:4], DK_SCALE, None, ALU.mult)
                    dve.drain()
                    TT(gfac[:, 2:4], gfac[:, 0:2], gnorm[:, 0:2], ALU.mult)
                    dve.drain()
                    TS(gfac[:, 4:6], gfac[:, 2:4], -1.0, None, ALU.mult)
                    dve.wait_ge(ga_w, ga0 + 1)
                    dve.wait_ge(gb_r, gb0 + 3)
                    for a in range(2):
                        STT(am[:, a, :], GA[:, a * P:(a + 1) * P], gfac[:, 2 + a:3 + a], dec_s[:, a, :],
                            ALU.mult, ALU.mult)
                    TT(kx[:, :], GA[:, 2 * P:3 * P], dec_t[:, 1, :], ALU.mult).then_inc(ga_r, 1)
                    dve.drain()
                    level_mask(0, xm[0])
                    ahead(7)
                    dve.wait_ge(ga_w, ga0 + 2)
                    TT(g_att[:, :, :].rearrange("p a n -> p (a n)"), GA[:, 0:3 * P],
                       dec_t[:, :, :].rearrange("p a n -> p (a n)"), ALU.mult)
                    dve.drain().then_inc(ga_r, 1)
                    ahead(8)
                    TT(tt[:, 0:2, :], ident.unsqueeze(1).to_broadcast([P, 2, P]), xm[0][:, :, :], ALU.subtract)
                    level_mask(1, xm[1])
                    dve.wait_ge(ga_w, ga0 + 3)
                    STT(tt[:, 2:4, :], GA[:, 0:2 * P].rearrange("p (a n) -> p a n", a=2), -1.0,
                        ident.unsqueeze(1).to_broadcast([P, 2, P]), ALU.mult, ALU.add)
                    dve.drain().then_inc(ga_r, 1)
                    dve.wait_ge(sincos_ready, n1)
                    s5_turn(0)
                    ahead(9)
                    nc.vector.reciprocal(hsig[:, 1, :], hsig[:, 1, :])
                    s5_add(0)
                    dve.wait_ge(hgrn_used, n1)
                    lb0, lb1 = (lb[:, ds(u, 1), c:c + 1].rearrange("p a b -> p (a b)") for c in range(2))
                    TS(hf[:, :], hsig[:, 0, :], lb1, lb0, ALU.mult, ALU.add)
                    TS(hk[:, :], hsig[:, 1, :], lb1, None, ALU.mult)
                    dve.drain().then_inc(hsig_used, 1)
                    ahead(10)
                    invert(1)
                    dve.wait_ge(hq_staged, n1)
                    h_scores(0)
                    s5_turn(1)
                    ahead(11)
                    h_scores(1)
                    s5_add(1)
                    ahead(12)
                    invert(2)
                    h_scores(2)
                    ahead(13)
                    h_scores(3)
                    s5_scan(0)
                    ahead(14)
                    invert(3)
                    h_scores(4)
                    s5_scan(1)
                    ahead(15)
                    h_scores(5)
                    conv_taps(2)
                    ahead(16)
                    invert(4)
                    h_scores(6)
                    rope(0)
                    ahead(17)
                    h_scores(7)
                    s5_back(0)
                    ahead(18)
                    invert(5)
                    dve.wait_ge(ha_w, ha0 + 9)
                    CP(h_att[:, 1, :], HA[:, 0:P])
                    dve.drain().then_inc(ha_r, 1)
                    rope(1)
                    dve.drain().then_inc(roped, 1)
                    ahead(19)
                    s5_back(1)
                    dve.wait_ge(gb_w, gb0 + 4)
                    for a in range(2):
                        last = TS(vb[:, a, :], GB[:, a * P:(a + 1) * P], gfac[:, a:a + 1], None, ALU.mult)
                    last.then_inc(gb_r, 1)
                    dve.wait_ge(ret_in, n1 * 16)
                    dve.wait_ge(ra_w, ra0 + 2)
                    TT(r_att[:, 0:2, :].rearrange("p a n -> p (a n)"), RA[:, 0:2 * P], ret_decay[:, :], ALU.mult)
                    TT(r_att[:, 2, :], RA[:, 2 * P:3 * P], ret_decay[:, 0:P], ALU.mult)
                    dve.drain().then_inc(ra_r, 1)
                    ahead(20)
                    invert(6)
                    s5_back(2)
                    ahead(21)
                    dve.wait_ge(ga_w, ga0 + 16)
                    CP(vn[:, 0, :], GA[:, 0:P])
                    dve.drain().then_inc(ga_r, 1)
                    dve.wait_ge(ra_w, ra0 + 4)
                    for a in range(2):
                        nc.vector.bn_stats(r_st[:, a, :], RA[:, a * P:(a + 1) * P])
                    dve.drain()
                    for a in range(2):
                        nc.vector.bn_aggr(r_mv[:, a, :], r_st[:, a, :])
                    dve.drain()
                    TS(r_rs[:, :], r_mv[:, :, 1], EPS, None, ALU.add)
                    dve.drain().then_inc(r_var_ready, 1)
                    s5_back(3)
                    ahead(22)
                    dve.wait_ge(ga_w, ga0 + 17)
                    STT(vt[:, :], GA[:, 0:P], gfac[:, 5:6], vb[:, 1, :], ALU.mult, ALU.add)
                    dve.drain().then_inc(ga_r, 1)
                    dve.wait_ge(r_rs_ready, n1)
                    for a in range(2):
                        TS(r_o[:, a, :], RA[:, a * P:(a + 1) * P], r_mv[:, a, 0:1], r_rs[:, a:a + 1],
                           ALU.subtract, ALU.mult)
                    dve.drain().then_inc(ra_r, 1)
                    s5_back(4)
                    s5_back(5)
                    ahead(23)
                    dve.wait_ge(ga_w, ga0 + 18)
                    CP(vn[:, 1, :], GA[:, 0:P])
                    dve.drain().then_inc(ga_r, 1)
                    dve.wait_ge(ha_w, ha0 + 11)
                    dve.wait_ge(hz_staged, n1)
                    finish(1, HA, V_HNW).then_inc(ha_r, 1)
                    ahead(24)
                    dve.wait_ge(sa_w, sa0 + 4)
                    STT(yT[:, 2, ds(u, 1), :].rearrange("p a n -> p (a n)"), s_u[:, :],
                        vec[:, ds(u + V_S5D, 1)], SA[:, 0:SEQ], ALU.mult, ALU.add).then_inc(sa_r, 1)
                    dve.drain().then_inc(s5_used, 1)
                    ahead(25)
                    dve.wait_ge(ga_w, ga0 + 20)
                    dve.wait_ge(gz_staged, n1)
                    finish(0, GA, V_GNW).then_inc(ga_r, 1)
                    dve.wait_ge(ra_w, ra0 + 5)
                    dve.wait_ge(rz_staged, n1)
                    finish(3, RA, None).then_inc(ra_r, 1)
                    ahead(26)
                    s5_phases(*(ds(l * STATE_TILES + u * ST + (ST + j), 1) for j in range(ST)))
                    dve.drain().then_inc(units_done, 1)
                    ahead(27)

                def y_low(m):
                    dve.wait_ge(y_hi_ready, l * N_BRANCH + (m + 1))
                    hi, lo = y_parts(MERGE_ORDER[m])
                    for k in range(0, UNITS, 4):
                        last = TT(lo[:, k:k + 4, :], y_whole(MERGE_ORDER[m])[:, k:k + 4, :], hi[:, k:k + 4, :].bitcast(f32),
                                  ALU.subtract)
                    last.then_inc(y_lo_ready, 1)

                y_low(0)
                y_low(1)
                with dve.Fori(0, UNITS // 2) as v:
                    n = dve.snap(l * UNITS + v * 2)
                    for i in range(2):
                        zv = zs[:, ds(v * 2 + i, 1), :].rearrange("p a n -> p (a n)")
                        yv = yT[:, 2, ds(v * 2 + i, 1), :].rearrange("p a n -> p (a n)")
                        dve.wait_ge(glu_sig, n + (i + 3))
                        TT(zv, zv, glu_s[i][:, :], ALU.mult)
                        dve.drain()
                        TT(zv, zv, yv, ALU.mult).then_inc(glu_done, 1)
                y_low(2)
                y_low(3)
                with dve.Fori(0, MT) as t:
                    n = dve.snap((l * MT + t) * N_BRANCH)
                    s0 = dve.snap(sl + MERGE_SPLIT0 + t * MERGE_HALVES)
                    mv = merged[:, ds(t, 1), :].rearrange("p a n -> p (a n)")
                    for pair in range(2):
                        for i in range(6 * pair, 6 * pair + 4):
                            split_lo(i + RING, s0)
                        for m in (2 * pair, 2 * pair + 1):
                            i = 6 * pair + 4 + m % 2
                            dve.wait_ge(split_used, s0 + (i + 1 + RING))
                            dve.wait_ge(gate_r, n + (m + 3))
                            src = (SA, SB)[m % 2][:, 0:SEQ]
                            if m == 0:
                                TT(mv, src, gate_s[m % 2], ALU.mult)
                            else:
                                TT(gated[:, :], src, gate_s[m % 2], ALU.mult)
                                dve.drain()
                                TT(mv, mv, gated[:, :], ALU.add)
                            dve.drain().then_inc(br_r, 1)
                            split_lo(i + RING, s0)
                dve.drain().then_inc(params_used, 1)
                for c in range(4):
                    dve.wait_ge(merged_hi, l * 4 + (c + 1))
                    low_part(c, merged).then_inc(merged_lo, 1)

                def residual(t, i, s0):
                    dve.wait_ge(split_used, s0 + (2 * i + 2 + RING))
                    xv = xT[:, ds(t * OUT_TILES + i, 1), :].rearrange("p a n -> p (a n)")
                    TT(xv, xv, PJ[i % 2][:, 0:SEQ], ALU.add).then_inc(out_r, 1)

                with dve.Fori(0, OUT_PASSES - 1) as t:
                    s0 = dve.snap(sl + OUT_SPLIT0 + t * RING)
                    for i in range(OUT_TILES):
                        residual(t, i, s0)
                        for j in range(2 * i, 2 * i + 2):
                            split_lo(RING + j, s0)
                s0 = dve.snap(sl + (OUT_SPLIT0 + (OUT_PASSES - 1) * RING))
                last_pass = dve.snap(l * 0 + (OUT_PASSES - 1))
                for i in range(OUT_TILES):
                    residual(last_pass, i, s0)
                dve.drain().then_inc(x_ready, 1)
            dve.wait_ge(ms_written, DEPTH + 1)
            mean_square()
            diagonal(DEPTH + 1)
            for k in range(KT):
                last = STT(h_last[:, k, :], xT[:, k, :], vec[:, V_FNW + k:V_FNW + k + 1], GA[:, 0:SEQ], ALU.mult, ALU.mult)
            last.then_inc(h_ready, 1)
            for i in range(2 * KT // 4):
                a, k = i // (KT // 4), i % (KT // 4)
                dve.wait_ge(xT_written, KT // 2 + i + 1)
                CP(x_tok[:, a, k * 512:(k + 1) * 512], (GA, GB)[i % 2][:, :]).then_inc(xT_read, 1)

        @block.tensor
        def _(pe):
            def MM(o, w, m, start=True, stop=True):
                return nc.tensor.matmul(o, w, m, start=start, stop=stop)

            TR = nc.tensor.transpose
            pe.wait_ge(consts_in, 16 * 6)
            pe.wait_ge(x_in, 32)
            for k in range(KT // 2):
                if k > 1:
                    pe.wait_ge(xT_read, k - 1)
                for j in range(2):
                    for a in range(2):
                        last = TR((GA, GB)[k % 2][:, j * SEQ + a * P:j * SEQ + (a + 1) * P],
                                  x_tok[:, a, (2 * k + j) * P:(2 * k + j + 1) * P], ident)
                last.then_inc(xT_written, 1)
            pe.wait_ge(s5_rows_ready, 1)
            for a in range(4):
                last = MM(RA[:, a * STATE_ROWS:(a + 1) * STATE_ROWS], s5_rows[:, a, :],
                          ident[0:STATE_ROWS, 0:STATE_ROWS])
            last.then_inc(s5_rowsT, 1)

            def sum_squares(n):
                pe.wait_ge(sq_ready, n)
                for a in range(2):
                    for k in range(KT):
                        last = MM(GA[:, a:a + 1], squares[:, k, a * P:(a + 1) * P], ones[:, 0:1], k == 0, k == KT - 1)
                last.then_inc(ms_written, 1)

            def spread_rms(n):
                pe.wait_ge(diag_ready, n)
                MM(GA[:, 0:SEQ], ones[:, :], am[:, :, :].rearrange("p a n -> p (a n)")).then_inc(rms_spread, 1)

            def three_pass(o, w, k, h, first, last):
                (wh, wl), (mh, ml) = w(k), h(k)
                MM(o, wh, mh, first, False)
                MM(o, wh, ml, False, False)
                return MM(o, wl, mh, False, last)

            with pe.Fori(0, DEPTH) as l:
                l1 = pe.snap(l + 1)
                sl, rl = pe.snap(l * SPLITS), pe.snap(l * RAW_USES)
                pe.wait_ge(params_in, l1 * (16 * 12))
                pe.wait_ge(x_ready, l1)
                TR(GB[:, 0:V_ROWS], vec_rows[:, :], ident[0:V_ROWS, 0:V_ROWS]).then_inc(vec_rowsT, 1)
                sum_squares(l1)
                spread_rms(l1)
                pe.wait_ge(s5_par_ready, 1)
                for a in range(2):
                    for k in range(KT):
                        if a == 0 and k % 4 == 0:
                            pe.wait_ge(h_full_ready, l * 4 + (k // 4 + 1))
                        last = MM(RA[:, a * 2 * UNITS:(a + 1) * 2 * UNITS], h_full[:, k, a * P:(a + 1) * P],
                                  w_ab[:, k, :], k == 0, k == KT - 1)
                last.then_inc(ab_written, 1)
                pe.wait_ge(g_ready, l1)
                MM(RA[:, 0:2 * UNITS], upto, gate_g[:, :, :].rearrange("p a u -> p (a u)"))
                MM(RA[:, 2 * UNITS:3 * UNITS], after, gate_g[:, 0, :]).then_inc(gc_written, 1)
                with pe.Fori(0, UNITS) as u:
                    n = pe.snap(l * UNITS + u)
                    n1 = pe.snap(n + 1)
                    pj0, ga0, gb0, ha0 = pe.snap(n * NB), pe.snap(n * GA_N), pe.snap(n * GB_N), pe.snap(n * HA_N)
                    ra0, sa0, cv0 = pe.snap(n * RA_N), pe.snap(n * SA_N), pe.snap(n * 3)
                    r0 = pe.snap(rl + u * USES)

                    def project(i):
                        b, h = i // 2, i % 2
                        o = PJ[b % 2]
                        if h == 0:
                            pe.wait_ge(pj_read, pj0 + (b + 1))

                        def is_split(j):
                            pe.wait_ge(raw_used[j % RING], r0 + (j // RING + 2))

                        is_split(i)
                        for k in range(HALF):
                            last = three_pass(o[:, 0:SEQ], lambda k: (w_hi[i % RING][:, k, :], w_lo[i % RING][:, k, :]),
                                              k, lambda k: (h_hi[:, h * HALF + k, :], h_lo[:, h * HALF + k, :]),
                                              h == 0 and k == 0, h == 1 and k == HALF - 1)
                        last.then_inc(split_used, 1)

                    def gdn_bank(stage):
                        pe.wait_ge(ga_r, ga0 + (stage + 1))

                    def g_decay_t():
                        pe.wait_ge(cols_ready, l1)
                        pe.wait_ge(gcols_ready, n1)
                        pe.wait_ge(gb_r, gb0 + 1)
                        MM(GB[:, 0:P], ident, mask_dt, True, False)
                        MM(GB[:, 0:P], g_bc[:, 0, :], upto, False, True)
                        MM(GB[:, P:2 * P], g_bc[:, 1, :], upto)
                        MM(GB[:, 2 * P:3 * P], ident, mask_dt, True, False)
                        MM(GB[:, 2 * P:3 * P], g_bc[:, 1, :], upto, False, True).then_inc(gb_w, 1)

                    def g_decay_s():
                        pe.wait_ge(gb_r, gb0 + 2)
                        for a in range(2):
                            MM(GB[:, a * P:(a + 1) * P], ident, mask_ds, True, False)
                            last = MM(GB[:, a * P:(a + 1) * P], g_bc[:, a, :], neg_upto, False, True)
                        last.then_inc(gb_w, 1)

                    def g_norms():
                        pe.wait_ge(conv_done, cv0 + 2)
                        pe.wait_ge(gb_r, gb0 + 3)
                        for m, t in enumerate((gk2, gq2)):
                            for a in range(2):
                                last = MM(GB[:, 2 * m + a:2 * m + a + 1], t[:, a * P:(a + 1) * P], ones[:, 0:1])
                        last.then_inc(gb_w, 1)

                    def g_gram_k():
                        gdn_bank(0)
                        for a in range(2):
                            MM(GA[:, a * P:(a + 1) * P], gk[:, a * P:(a + 1) * P], gk[:, a * P:(a + 1) * P])
                        MM(GA[:, 2 * P:3 * P], gk[:, 0:P], gk[:, P:2 * P]).then_inc(ga_w, 1)

                    def g_values():
                        pe.wait_ge(conv_done, cv0 + 3)
                        pe.wait_ge(gb_r, gb0 + 4)
                        for a in range(2):
                            last = TR(GB[:, a * P:(a + 1) * P], gv[:, a * P:(a + 1) * P], ident)
                        last.then_inc(gb_w, 1)

                    def g_gram_q():
                        gdn_bank(1)
                        MM(GA[:, 0:2 * P], gk[:, 0:P], gq[:, :])
                        MM(GA[:, 2 * P:3 * P], gk[:, P:2 * P], gq[:, P:2 * P]).then_inc(ga_w, 1)

                    def g_first():
                        gdn_bank(2)
                        for a in range(2):
                            last = MM(GA[:, a * P:(a + 1) * P], xm[0][:, a, :], ident)
                        last.then_inc(ga_w, 1)

                    def g_tx(s):
                        gdn_bank(3 + 2 * (s - 1))
                        for a in range(2):
                            last = MM(GA[:, a * P:(a + 1) * P], xm[s % 2][:, a, :], tt[:, 2 + a, :])
                        last.then_inc(ga_w, 1)

                    def g_txt(s):
                        gdn_bank(4 + 2 * (s - 1))
                        for a in range(2):
                            if s + 1 < LEVELS:
                                MM(GA[:, a * P:(a + 1) * P], rr[:, a, :], tt[:, a, :])
                            last = MM(GA[:, (2 + a) * P:(3 + a) * P], tt[:, a, :], rr[:, a, :])
                        last.then_inc(ga_w, 1)

                    def g_new0():
                        gdn_bank(15)
                        MM(GA[:, 0:P], tt[:, 2, :], vb[:, 0, :]).then_inc(ga_w, 1)

                    def g_cross():
                        gdn_bank(16)
                        MM(GA[:, 0:P], kx[:, :], vn[:, 0, :]).then_inc(ga_w, 1)

                    def g_new1():
                        gdn_bank(17)
                        MM(GA[:, 0:P], tt[:, 3, :], vt[:, :]).then_inc(ga_w, 1)

                    def attend(o, att, val):
                        MM(o[:, 0:P], att[:, 0, :], val[:, 0, :])
                        MM(o[:, P:2 * P], att[:, 1, :], val[:, 0, :], True, False)
                        return MM(o[:, P:2 * P], att[:, 2, :], val[:, 1, :], False, True)

                    def to_channels(o, src, used):
                        TR(o[:, 0:P], src[:, 0, :], ident).then_inc(used, 1)
                        return TR(o[:, P:2 * P], src[:, 1, :], ident)

                    def g_out():
                        gdn_bank(18)
                        attend(GA, g_att, vn).then_inc(ga_w, 1)

                    def g_turn():
                        gdn_bank(19)
                        to_channels(GA, g_o, gdn_qkv_used).then_inc(ga_w, 1)

                    def s_turn():
                        pe.wait_ge(bc_padded, n1)
                        pe.wait_ge(sa_r, sa0 + 1)
                        for a in range(4):
                            last = TR(SA[:, a * P:(a + 1) * P], bc_pad[:, a, :], ident)
                        last.then_inc(sa_w, 1)

                    def s_bu(half):
                        pe.wait_ge(u_staged, n1)
                        pe.wait_ge(sa_r, sa0 + (2 + half))
                        for i in range(2):
                            j = 2 * half + i
                            rows_ = slice(32 * j, 32 * j + 32)
                            first = MM(S2[:, i, 0:SEQ], bc_T[rows_, 0, :], s_u[rows_, :])
                            if half == 0 and i == 0:
                                first.then_inc(bc_used, 1)
                            last = MM(S2[:, i, SEQ:2 * SEQ], bc_T[rows_, 1, :], s_u[rows_, :])
                        last.then_inc(sa_w, 1)

                    def s_cx():
                        pe.wait_ge(x_re_im_ready, n1)
                        pe.wait_ge(sa_r, sa0 + 4)
                        for j in range(ST):
                            rows_ = slice(32 * j, 32 * j + 32)
                            MM(SA[rows_, 0:SEQ], bc_T[:, 2, rows_], s5_p[:, j, :], True, False)
                            last = MM(SA[rows_, 0:SEQ], bc_T[:, 3, rows_], s5_q[:, j, :], False, True)
                        last.then_inc(sa_w, 1)

                    def h_pairs(stage):
                        if stage == 0:
                            pe.wait_ge(hq_staged, n1)
                            pe.wait_ge(hsig_used, n1 + 1)
                        pe.wait_ge(ha_r, ha0 + (stage + 1))
                        for a in range(2):
                            last = MM(HA[:, a * P:(a + 1) * P], hk[:, a * P:(a + 1) * P], hq[:, a * P:(a + 1) * P])
                        last.then_inc(ha_w, 1)

                    def h_cross():
                        pe.wait_ge(ha_r, ha0 + 9)
                        MM(HA[:, 0:P], hk[:, 0:P], hq[:, P:2 * P]).then_inc(ha_w, 1)

                    def h_out():
                        pe.wait_ge(hv_staged, n * 2 + 2)
                        pe.wait_ge(ha_r, ha0 + 10)
                        attend(HA, h_att, hv).then_inc(ha_w, 1)

                    def h_turn():
                        pe.wait_ge(ha_r, ha0 + 11)
                        to_channels(HA, h_o, hgrn_used).then_inc(ha_w, 1)

                    def values(val, staged, stage):
                        pe.wait_ge(staged, n * 2 + 1)
                        pe.wait_ge(ra_r, ra0 + stage)
                        for a in range(2):
                            last = TR(RA[:, a * P:(a + 1) * P], val[:, a, :], ident)
                        last.then_inc(ra_w, 1)

                    def r_scores():
                        pe.wait_ge(roped, n1)
                        pe.wait_ge(ra_r, ra0 + 2)
                        MM(RA[:, 0:2 * P], rx[1][:, 0:P], rx[0][:, :])
                        MM(RA[:, 2 * P:3 * P], rx[1][:, P:2 * P], rx[0][:, P:2 * P]).then_inc(ra_w, 1)

                    def r_out():
                        pe.wait_ge(rv_staged, n * 2 + 2)
                        pe.wait_ge(ra_r, ra0 + 4)
                        attend(RA, r_att, rv).then_inc(ra_w, 1)

                    def r_turn():
                        pe.wait_ge(ra_r, ra0 + 5)
                        to_channels(RA, r_o, ret_used).then_inc(ra_w, 1)

                    pe.wait_ge(h_ready, l1 * 4)
                    project(0)
                    project(1)
                    g_decay_t()
                    project(2)
                    g_decay_s()
                    project(3)
                    project(4)
                    s_turn()
                    project(5)
                    project(6)
                    project(7)
                    g_norms()
                    g_gram_k()
                    project(8)
                    s_bu(0)
                    g_gram_q()
                    project(9)
                    g_first()
                    project(10)
                    g_tx(1)
                    s_bu(1)
                    project(11)
                    g_txt(1)
                    h_pairs(0)
                    project(12)
                    g_tx(2)
                    h_pairs(1)
                    project(13)
                    g_txt(2)
                    h_pairs(2)
                    project(14)
                    values(hv, hv_staged, 1)
                    g_tx(3)
                    h_pairs(3)
                    project(15)
                    g_txt(3)
                    h_pairs(4)
                    project(16)
                    g_tx(4)
                    h_pairs(5)
                    project(17)
                    g_txt(4)
                    h_pairs(6)
                    project(18)
                    g_tx(5)
                    h_pairs(7)
                    g_values()
                    project(19)
                    g_txt(5)
                    h_cross()
                    project(20)
                    g_tx(6)
                    r_scores()
                    project(21)
                    g_txt(6)
                    h_out()
                    values(rv, rv_staged, 3)
                    project(22)
                    g_new0()
                    r_out()
                    project(23)
                    g_cross()
                    project(24)
                    g_new1()
                    h_turn()
                    project(25)
                    g_out()
                    r_turn()
                    s_cx()
                    project(26)
                    g_turn()
                    project(27)

                pj_last = pe.snap(l1 * (UNITS * NB) + 2)

                with pe.Fori(0, UNITS // 2) as v:
                    n = pe.snap(l * UNITS + v * 2)
                    filled = pe.snap((l * (UNITS // 2) + v + 1) * 16)
                    pe.wait_ge(gelu_done, l1)
                    pe.wait_ge(pj_read, pj_last)
                    for i in range(2):
                        pe.wait_ge(glu_sig, n + (i + 1))
                        pe.wait_ge(glu_full[i], filled)
                        for k in range(KB):
                            last = MM(PJ[i][:, 0:SEQ], glu_w[i][:, k, :], yT[:, 2, k, :], k == 0, k == KB - 1)
                        last.then_inc(glu_used, 1)
                units_all = pe.snap(l1 * UNITS)
                with pe.Fori(0, MT) as t:
                    r0 = pe.snap(rl + UNITS * USES + t * MERGE_USES)
                    n = pe.snap((l * MT + t) * N_BRANCH)
                    pe.wait_ge(glu_sig, units_all + 2)
                    for pair in range(2):
                        for m in (2 * pair, 2 * pair + 1):
                            pe.wait_ge(gate_r, n + (m + 1))
                            for h in range(2):
                                j = 6 * pair + 2 * (m % 2) + h
                                pe.wait_ge(raw_used[j % RING], r0 + (j // RING + 2))
                                for k in range(HALF):
                                    last = three_pass(
                                        PJ[m % 2][:, 0:SEQ],
                                        lambda k: (w_hi[j % RING][:, k, :], w_lo[j % RING][:, k, :]), k,
                                        lambda k: (h_hi[:, h * HALF + k, :], h_lo[:, h * HALF + k, :]),
                                        h == 0 and k == 0, h == 1 and k == HALF - 1)
                                last.then_inc(split_used, 1)
                        for m in (2 * pair, 2 * pair + 1):
                            j = 6 * pair + 4 + m % 2
                            pe.wait_ge(raw_used[j % RING], r0 + (j // RING + 2))
                            pe.wait_ge(br_r, n + (m + 1))
                            pe.wait_ge(y_lo_ready, l * N_BRANCH + (m + 1))
                            hi, lo = y_parts(MERGE_ORDER[m])
                            for k in range(KB):
                                last = three_pass(
                                    (SA, SB)[m % 2][:, 0:SEQ],
                                    lambda k: (w_hi[j % RING][:, k, :], w_lo[j % RING][:, k, :]), k,
                                    lambda k: (hi[:, k, :], lo[:, k, :]), k == 0, k == KB - 1)
                            last.then_inc(split_used, 1)
                with pe.Fori(0, OUT_PASSES) as t:
                    r0 = pe.snap(rl + (UNITS * USES + MT * MERGE_USES) + t)
                    n = pe.snap((l * OUT_PASSES + t) * OUT_TILES)
                    for i in range(OUT_TILES):
                        pe.wait_ge(out_r, n + (i + 1))
                        for h in range(2):
                            j = 2 * i + h
                            pe.wait_ge(raw_used[j], r0 + 2)
                            for k in range(HALF):
                                if k % 4 == 0:
                                    pe.wait_ge(merged_lo, l * 4 + (2 * h + k // 4 + 1))
                                last = three_pass(
                                    PJ[i][:, 0:SEQ], lambda k: (w_hi[j][:, k, :], w_lo[j][:, k, :]), k,
                                    lambda k: (h_hi[:, h * HALF + k, :], h_lo[:, h * HALF + k, :]),
                                    h == 0 and k == 0, h == 1 and k == HALF - 1)
                            last.then_inc(split_used, 1)
            sum_squares(DEPTH + 1)
            spread_rms(DEPTH + 1)
            pe.wait_ge(h_ready, DEPTH * 4 + 1)
            for i in range(2 * KT // 4):
                a, k = i // (KT // 4), i % (KT // 4)
                pe.wait_ge(xT_read, KT // 2 + max(i - 1, 0))
                for j in range(4):
                    last = TR((GA, GB)[i % 2][:, j * P:(j + 1) * P], h_last[:, 4 * k + j, a * P:(a + 1) * P], ident)
                last.then_inc(xT_written, 1)


OUT_NAMES = ["out"]


def kernel(**inputs):
    import concourse.bacc as bacc
    from concourse.bass_utils import run_bass_kernel_spmd

    nc = bacc.Bacc("TRN2", target_bir_lowering=False, num_devices=1, dynamic_dma_scratch_size=4096)
    arrays = {name: np.ascontiguousarray(inputs[name]) for name in INPUTS}
    arrays.update(shape_constants())
    args = {name: nc.dram_tensor(name, a.shape, mybir.dt.from_np(a.dtype), kind="ExternalInput").ap()
            for name, a in arrays.items()}
    out = nc.dram_tensor("out", (1, SEQ, D_MODEL), mybir.dt.float32, kind="ExternalOutput").ap()
    trunk_kernel(nc, args, out)
    got = run_bass_kernel_spmd(nc, [arrays], core_ids=[0])
    return got.results[0]["out"]
```
